# Optimizing a Trainium2 kernel written in Bass

```python
import jax, jax.numpy as jnp
from jax import lax
import numpy as np

D_MODEL = 1024
BATCH = 1
SEQ = 512
DEPTH = 1

D_MIX = D_MODEL
GLA_WIDTH = D_MIX // 2
GLA_HEADS = 4
GLA_DV = GLA_WIDTH // GLA_HEADS
GLA_DK = GLA_DV // 2
GLA_KW = GLA_HEADS * GLA_DK
GLA_GATE_RANK = 16
GLA_TAU = 16.0
GLA_CHUNK = 64
ATT_WIDTH = D_MIX - GLA_WIDTH
ATT_HEADS = 8
ATT_HD = ATT_WIDTH // ATT_HEADS
ROT_DIM = ATT_HD // 4
ROPE_THETA = 500000.0
DILATED_PATTERNS = ((128, 1), (512, 4), (2048, 16))
ATT_BLOCK = 128
D_FF = 2816
EPS = 1e-6
IN_SIZES = (GLA_KW, GLA_KW, GLA_WIDTH, GLA_WIDTH, GLA_GATE_RANK, ATT_WIDTH, ATT_WIDTH, ATT_WIDTH)
D_IN = GLA_KW * 2 + GLA_WIDTH * 2 + GLA_GATE_RANK + ATT_WIDTH * 3

kernel_name = "hymba_gla_dilated_macaron_layer"

def rms_norm(x, g):
    xf = x.astype(jnp.float32)
    y = xf * lax.rsqrt(jnp.mean(xf * xf, axis=-1, keepdims=True) + EPS)
    return (y * g.astype(jnp.float32)).astype(x.dtype)

def swiglu(x, w1, w3, w2):
    return (jax.nn.silu(x @ w1) * (x @ w3)) @ w2

def rope_tables(positions):
    inv_freq = ROPE_THETA ** (-jnp.arange(0, ROT_DIM, 2, dtype=jnp.float32) / ROT_DIM)
    ang = positions.astype(jnp.float32)[..., None] * inv_freq
    return jnp.cos(ang)[:, :, None, :], jnp.sin(ang)[:, :, None, :]

def rope_partial(t, cos, sin):
    half = ROT_DIM // 2
    cos = cos.astype(t.dtype)
    sin = sin.astype(t.dtype)
    t1 = t[..., :half]
    t2 = t[..., half:ROT_DIM]
    return jnp.concatenate([t1 * cos - t2 * sin, t2 * cos + t1 * sin, t[..., ROT_DIM:]], axis=-1)

def gla_chunked(q, k, v, log_a):
    B, H, S, dk = q.shape
    dv = v.shape[-1]
    n = S // GLA_CHUNK

    def chunks(t):
        return t.astype(jnp.float32).reshape(B, H, n, GLA_CHUNK, t.shape[-1])

    q, k, v, g = chunks(q), chunks(k), chunks(v), chunks(log_a)
    b = jnp.cumsum(g, axis=3)
    b_last = b[:, :, :, -1:, :]
    q_dec = q * jnp.exp(b)
    k_inv = k * jnp.exp(-b)
    k_tail = k * jnp.exp(b_last - b)
    causal = jnp.tril(jnp.ones((GLA_CHUNK, GLA_CHUNK), dtype=bool))
    a = jnp.where(causal, jnp.einsum('bhnid,bhnjd->bhnij', q_dec, k_inv), 0.0)
    o_intra = jnp.einsum('bhnij,bhnje->bhnie', a, v)
    u = jnp.einsum('bhnjd,bhnje->bhnde', k_tail, v)
    decay = jnp.exp(b_last[:, :, :, 0, :])

    def step(state, inp):
        dec_c, u_c = inp
        return dec_c[..., None] * state + u_c, state

    init = jnp.zeros((B, H, dk, dv), jnp.float32)
    _, s_prev = lax.scan(step, init, (jnp.moveaxis(decay, 2, 0), jnp.moveaxis(u, 2, 0)))
    s_prev = jnp.moveaxis(s_prev, 0, 2)
    o_inter = jnp.einsum('bhnid,bhnde->bhnie', q_dec, s_prev)
    return (o_intra + o_inter).reshape(B, H, S, dv)

def dilated_branch(q, k, v, window, dilation):
    B, H, S, hd = q.shape
    L = S // dilation
    span = window // dilation
    nb = -(-L // ATT_BLOCK)
    Lp = nb * ATT_BLOCK

    def to_blocks(t):
        t = t.reshape(B, H, L, dilation, hd).transpose(0, 1, 3, 2, 4)
        t = jnp.pad(t, ((0, 0), (0, 0), (0, 0), (0, Lp - L), (0, 0)))
        return t.reshape(B, H, dilation, nb, ATT_BLOCK, hd)

    qb, kb, vb = to_blocks(q), to_blocks(k), to_blocks(v)
    shift = ((0, 0), (0, 0), (0, 0), (1, 0), (0, 0), (0, 0))
    kk = jnp.concatenate([jnp.pad(kb[:, :, :, :-1], shift), kb], axis=4)
    vv = jnp.concatenate([jnp.pad(vb[:, :, :, :-1], shift), vb], axis=4)
    s = jnp.einsum('bhrnqd,bhrnkd->bhrnqk', qb, kk).astype(jnp.float32)
    blk = jnp.arange(nb)[:, None, None]
    qi = jnp.arange(ATT_BLOCK)[None, :, None] + ATT_BLOCK
    ki = jnp.arange(2 * ATT_BLOCK)[None, None, :]
    dist = qi - ki
    mask = (dist >= 0) & (dist <= span) & (blk * ATT_BLOCK + ki - ATT_BLOCK >= 0)
    s = jnp.where(mask, s, -jnp.inf)
    m = jnp.max(s, axis=-1, keepdims=True)
    p = jnp.exp(s - m)
    den = jnp.sum(p, axis=-1, keepdims=True)
    o = jnp.einsum('bhrnqk,bhrnkd->bhrnqd', p.astype(v.dtype), vv).astype(jnp.float32) / den
    lse = (m + jnp.log(den))[..., 0]
    o = o.reshape(B, H, dilation, Lp, hd)[:, :, :, :L].transpose(0, 1, 3, 2, 4).reshape(B, H, S, hd)
    lse = lse.reshape(B, H, dilation, Lp)[:, :, :, :L].transpose(0, 1, 3, 2).reshape(B, H, S)
    return o, lse

def dilated_attention(q, k, v):
    outs, lses = [], []
    for window, dilation in DILATED_PATTERNS:
        o, lse = dilated_branch(q, k, v, window, dilation)
        outs.append(o)
        lses.append(lse)
    w = jax.nn.softmax(jnp.stack(lses, axis=0), axis=0)
    return jnp.sum(w[..., None] * jnp.stack(outs, axis=0), axis=0)

def setup_inputs(seed: int = 0) -> dict:
    key = jax.random.key(seed)
    ks = jax.random.split(key, 20)
    f32 = jnp.float32

    def nrm(k, shape, fan_in):
        return jax.random.normal(k, shape, f32) * (fan_in ** -0.5)

    def gain(k, shape):
        return 1.0 + 0.02 * jax.random.normal(k, shape, f32)

    x = jax.random.normal(ks[0], (BATCH, SEQ, D_MODEL), f32)
    positions = jnp.broadcast_to(jnp.arange(SEQ, dtype=jnp.int32)[None, :], (BATCH, SEQ))
    return {
        "x": x,
        "positions": positions,
        "ffn1_norm": gain(ks[1], (DEPTH, D_MODEL)),
        "ffn1_w1": nrm(ks[2], (DEPTH, D_MODEL, D_FF), D_MODEL),
        "ffn1_w3": nrm(ks[3], (DEPTH, D_MODEL, D_FF), D_MODEL),
        "ffn1_w2": nrm(ks[4], (DEPTH, D_FF, D_MODEL), D_FF),
        "mix_norm": gain(ks[5], (DEPTH, D_MODEL)),
        "w_in": nrm(ks[6], (DEPTH, D_MODEL, D_IN), D_MODEL),
        "gla_w_a2": nrm(ks[7], (DEPTH, GLA_GATE_RANK, GLA_KW), GLA_GATE_RANK),
        "gla_b_a": 0.01 * jax.random.normal(ks[8], (DEPTH, GLA_KW), f32),
        "gla_out_norm": gain(ks[9], (DEPTH, GLA_WIDTH)),
        "att_out_norm": gain(ks[10], (DEPTH, ATT_WIDTH)),
        "w_out": nrm(ks[11], (DEPTH, D_MIX, D_MODEL), D_MIX),
        "ffn2_norm": gain(ks[12], (DEPTH, D_MODEL)),
        "ffn2_w1": nrm(ks[13], (DEPTH, D_MODEL, D_FF), D_MODEL),
        "ffn2_w3": nrm(ks[14], (DEPTH, D_MODEL, D_FF), D_MODEL),
        "ffn2_w2": nrm(ks[15], (DEPTH, D_FF, D_MODEL), D_FF),
        "final_norm": gain(ks[16], (D_MODEL,)),
    }

def reference(x, positions, ffn1_norm, ffn1_w1, ffn1_w3, ffn1_w2, mix_norm, w_in, gla_w_a2, gla_b_a,
              gla_out_norm, att_out_norm, w_out, ffn2_norm, ffn2_w1, ffn2_w3, ffn2_w2, final_norm):
    B, S, _ = x.shape
    cos, sin = rope_tables(positions)
    offsets = []
    acc = 0
    for size in IN_SIZES[:-1]:
        acc += size
        offsets.append(acc)

    for l in range(DEPTH):
        x = x + 0.5 * swiglu(rms_norm(x, ffn1_norm[l]), ffn1_w1[l], ffn1_w3[l], ffn1_w2[l])

        h = rms_norm(x, mix_norm[l])
        proj = h @ w_in[l]
        gq, gk, gv, gr, ga, aq, ak, av = jnp.split(proj, offsets, axis=-1)

        def heads(t, nh):
            return t.reshape(B, S, nh, -1).transpose(0, 2, 1, 3)

        log_a = jax.nn.log_sigmoid((ga @ gla_w_a2[l] + gla_b_a[l]).astype(jnp.float32)) / GLA_TAU
        o_gla = gla_chunked(heads(gq, GLA_HEADS) * (GLA_DK ** -0.5), heads(gk, GLA_HEADS),
                            heads(gv, GLA_HEADS), heads(log_a, GLA_HEADS))
        o_gla = rms_norm(o_gla, gla_out_norm[l].reshape(GLA_HEADS, 1, GLA_DV))
        o_gla = o_gla.transpose(0, 2, 1, 3).reshape(B, S, GLA_WIDTH).astype(x.dtype) * jax.nn.silu(gr)

        q = rope_partial(aq.reshape(B, S, ATT_HEADS, ATT_HD), cos, sin) * (ATT_HD ** -0.5)
        k = rope_partial(ak.reshape(B, S, ATT_HEADS, ATT_HD), cos, sin)
        v = av.reshape(B, S, ATT_HEADS, ATT_HD)
        o_att = dilated_attention(q.transpose(0, 2, 1, 3), k.transpose(0, 2, 1, 3), v.transpose(0, 2, 1, 3))
        o_att = o_att.transpose(0, 2, 1, 3).reshape(B, S, ATT_WIDTH)
        o_att = rms_norm(o_att, att_out_norm[l]).astype(x.dtype)

        x = x + jnp.concatenate([o_gla, o_att], axis=-1) @ w_out[l]

        x = x + 0.5 * swiglu(rms_norm(x, ffn2_norm[l]), ffn2_w1[l], ffn2_w3[l], ffn2_w2[l])

    return rms_norm(x, final_norm)


_drawn_inputs = setup_inputs


def setup_inputs(seed=0):
    import zlib

    import numpy as np

    out = dict(_drawn_inputs(seed))
    spreads = {}
    factors = {'ffn1_norm': 4.655,
     'gla_b_a': 25.91,
     'gla_out_norm': 156.916,
     'att_out_norm': 87.273,
     'ffn2_norm': 25.359,
     'final_norm': 23.348}
    for name, (base, spread) in spreads.items():
        noise = np.random.default_rng([zlib.crc32(name.encode()), seed]).standard_normal(out[name].shape)
        drawn = base * np.exp(spread * noise) if base else spread * noise
        out[name] = __import__('jax').numpy.asarray(drawn.astype(out[name].dtype))
    for name, factor in factors.items():
        out[name] = (out[name] * factor).astype(out[name].dtype)
    return out
```

```python
import math
from contextlib import ExitStack

import numpy as np

import concourse.bass as bass
from concourse import mybir

F32 = mybir.dt.float32
F32R = mybir.dt.float32r
I32 = mybir.dt.int32
U32 = mybir.dt.uint32
ALU = mybir.AluOpType
ACT = mybir.ActivationFunctionType

P = 128
D = 1024
S = 512
KC = D // P
ST = S // P
D_FF = 2816
FT = D_FF // P
PARTS = ((0, 12), (12, 22))
GLA_W, GLA_H, GLA_DV, GLA_DK, GLA_KW, GLA_RANK, CHUNK = 512, 4, 128, 64, 256, 16, 64
ATT_W, ATT_H, HD, ROT = 512, 8, 64, 16
NCH = S // CHUNK
EPS = 1e-6
THETA = 500000.0
PATTERNS = ((128, 1), (512, 4), (2048, 16))

GQ, GK, GV, GR, GA, AQ, AK, AV = 0, 256, 512, 1024, 1536, 1552, 2064, 2576
T_AQ, T_AK, T_GQ, T_GK, T_GR, T_GA = 0, 4, 8, 10, 12, 16

UP_W, A_W, V_W = 2 * D, 2 * D, 4 * S
FFN_UNITS = FT + 2 * KC
FFN_TILES = 2 * FT + 2 * KC
MIX_UNITS = 1 + 8 + 4 + 4
MIX_TILES = 1 + 16 + 8 + 8
OUT_BANKS = (6, 1, 2, 3)
BANK_CREDIT = 4

G_FFN1, G_MIX, G_FFN2, G_FINAL, G_GLA, G_ATT, G_BA = 0, 8, 16, 24, 32, 36, 40
N_GAINS = 42

C_ID, C_ONE, C_STRIP, C_TRI, C_SCAN, C_FREQ, C_SGN = 0, 128, 256, 768, 1280, 1792, 1793
N_CONST = 1794
NORM = {0: 0, 2: 8}
MAGIC = 1.5 * 2.0 ** 23
TWO_PI = (6.28125, 0.00193500518798828125, 2 * math.pi - 6.28125 - 0.00193500518798828125)
SCORE_SCALE = HD ** -0.5
FAR = -1e30


def layer_program(nc, xT_in, positions, gains_in, up1, down1, w_proj, w_ga, w_v, w_a2, w_o, up2, down2,
                  const_in, outT):
    ctx = ExitStack()
    with ctx:
        def sb(name, shape, dt=F32, scope=ctx):
            return scope.enter_context(nc.sbuf_tensor(name, shape, dt))

        def sem(name):
            return ctx.enter_context(nc.semaphore(name))

        x = sb("x", [P, KC, S])
        h_hi = sb("h_hi", [P, KC, S], F32R)
        h_lo = sb("h_lo", [P, KC, S], F32R)
        raw = [sb(f"raw{j}", [P, UP_W]) for j in range(2)]
        w_hi = [sb(f"w_hi{j}", [P, UP_W], F32R) for j in range(2)]
        w_lo = [sb(f"w_lo{j}", [P, UP_W], F32R) for j in range(2)]
        const = sb("const", [P, N_CONST])
        gains = sb("gains", [P, N_GAINS, 1])
        credit = sb("credit", [P, 1])
        wa2 = sb("wa2", [GLA_RANK, GLA_KW])
        rstd = sb("rstd", [P, S])
        rstd_tok = sb("rstd_tok", [P, ST])
        sumsq = sb("sumsq", [P, S])
        square = sb("square", [P, S])
        rope_c = sb("rope_c", [P, S])
        rope_s = sb("rope_s", [P, S])
        head_rstd = (rope_c, rope_s)
        ident = const[:, C_ID:C_ID + P]
        ones = const[:, C_ONE:C_ONE + P]

        def ffn_memory(n):
            scope = ExitStack()
            g_hi = sb(f"g_hi{n}", [P, PARTS[0][1], S], F32R, scope)
            g_lo = sb(f"g_lo{n}", [P, PARTS[0][1], S], F32R, scope)
            gate = sb(f"gate{n}", [P, S], F32, scope)
            prod = sb(f"prod{n}", [P, S], F32, scope)
            scope.close()
            return g_hi, g_lo, gate, prod

        ffn_mem = {1: ffn_memory(1)}
        mix = ExitStack()
        projT = sb("projT", [P, 17, S], F32, mix)
        v_att = sb("v_att", [P, ST, ATT_W], F32, mix)
        v_gla = sb("v_gla", [P, ST, GLA_W], F32, mix)
        gt = [[sb(f"gt{n}_{p}", [P, S], F32, mix) for p in range(2)] for n in range(3)]
        mx = sb("mx", [P, 4 * ATT_H], F32, mix)
        negm = sb("negm", [P, 4 * ATT_H], F32, mix)
        den = sb("den", [P, 4 * ATT_H], F32, mix)
        rden = sb("rden", [P, 4 * ATT_H], F32, mix)
        late = ExitStack()
        probs = [sb(f"probs{j}", [P, 10 * P], F32, late) for j in range(2)]
        probsT = [sb(f"probsT{j}", [P, ST, S], F32, late) for j in range(2)]
        NDIAG = 8
        diag = sb("diag", [P, NDIAG, P], F32, late)
        late.close()
        late = ExitStack()
        k_tok = [sb(f"k_tok{p}", [P, ST, P], F32, late) for p in range(2)]
        state = [sb(f"state{p}", [P, NCH, GLA_DV], F32, late) for p in range(2)]
        att_g = [sb(f"att_g{j}", [P, S], F32, late) for j in range(2)]
        late.close()
        mix.close()
        ffn_mem[2] = ffn_memory(2)
        early = ExitStack()
        sb("under_ffn1", [P, 2 * PARTS[0][1] * S + 2 * S], F32, early)
        pos_i = sb("pos_i", [P, S], I32, early)
        ang = sb("ang", [P, S], F32, early)
        turn = sb("turn", [P, S], F32, early)
        part = sb("part", [P, S], F32, early)
        early.close()

        ps = [ctx.enter_context(nc.psum_tensor(f"bank{b}", [P, S], F32)) for b in range(8)]

        x_in = [sem(f"x_in{j}") for j in range(2)]
        const_landed = sem("const_landed")
        pos_landed = sem("pos_landed")
        w_in = [sem(f"w_in{j}") for j in range(2)]
        w_round = sem("w_round")
        w_split = sem("w_split")
        tile_done = sem("tile_done")
        tile_out = sem("tile_out")
        v_half = sem("v_half")
        h_round = sem("h_round")
        h_ready = sem("h_ready")
        sq_done = sem("sq_done")
        sq_added = sem("sq_added")
        sums_done = sem("sums_done")
        sums_out = sem("sums_out")
        root_done = sem("root_done")
        rstd_done = sem("rstd_done")
        silu_done = sem("silu_done")
        g_mul = sem("g_mul")
        g_round = sem("g_round")
        g_ready = sem("g_ready")
        pool_step = sem("pool_step")
        ang_sin = sem("ang_sin")
        rope_tab = sem("rope_tab")
        sgn_done = sem("sgn_done")
        rope_shuf = sem("rope_shuf")
        rope_cos = sem("rope_cos")
        rope_sin = sem("rope_sin")
        rope_done = sem("rope_done")
        z_done = sem("z_done")
        z_out = sem("z_out")
        act_step = sem("act_step")
        log_done = sem("log_done")
        gr_done = sem("gr_done")
        s_done = sem("s_done")
        s_masked = sem("s_masked")
        negm_done = sem("negm_done")
        exp_done = sem("exp_done")
        rden_done = sem("rden_done")
        diag_done = sem("diag_done")
        pt_done = sem("pt_done")
        pt_out = sem("pt_out")
        o_done = sem("o_done")
        o_out = sem("o_out")
        dve_step = sem("dve_step")
        b_done = sem("b_done")
        eb_done = sem("eb_done")
        tail_done = sem("tail_done")
        et_done = sem("et_done")
        gla_ready = sem("gla_ready")
        ktail_done = sem("ktail_done")
        ktail_out = sem("ktail_out")
        att_squares = sem("att_squares")
        ag_done = sem("ag_done")
        ag_out = sem("ag_out")
        u_done = sem("u_done")
        state_done = sem("state_done")
        og_done = sem("og_done")
        og_out = sem("og_out")
        att_scaled = sem("att_scaled")
        gla_scaled = sem("gla_scaled")
        fin_done = sem("fin_done")
        stored = sem("stored")

        block = ctx.enter_context(nc.Block())

        U_MIX, U_FFN2 = FFN_UNITS, FFN_UNITS + MIX_UNITS
        T_MIX, T_FFN2 = FFN_TILES, FFN_TILES + MIX_TILES
        N_UNITS = 2 * FFN_UNITS + MIX_UNITS

        def ffn_phases(u0, t0):
            out = []
            for a, b in PARTS:
                out.append(("up", u0, t0, b - a, a))
                u0, t0 = u0 + b - a, t0 + 2 * (b - a)
                out.append(("down", u0, t0, KC, a))
                u0, t0 = u0 + KC, t0 + KC
            return out

        def hidden(phase):
            return next(b - a for a, b in PARTS if a == phase[4])

        def unit_size(u):
            for base in (0, U_FFN2):
                if base <= u < base + FFN_UNITS:
                    for kind, u0, _, n, a in ffn_phases(base, 0):
                        if u0 <= u < u0 + n:
                            return UP_W if kind == "up" else P * next(b - c for c, b in PARTS if c == a)
            return D if u == U_MIX else UP_W

        @block.sync
        def _(sp):
            def load(u, i, src):
                if not (isinstance(i, int) and u + 2 * i < 2):
                    sp.wait_ge(w_split, u - 1 + 2 * i)
                sp.dma_start(raw[u % 2][:, 0:src.shape[-1]], src).then_inc(w_in[u % 2], 16)

            def phase(u0, n, source):
                peeled = u0 == 0
                if peeled:
                    for j in range(2):
                        load(j, 0, source(j))
                with sp.Fori(int(peeled), n // 2) as i:
                    for j in range(2):
                        load(u0 + j, i, source(2 * i + j))

            def ffn(base, up, down):
                for kind, u0, _, n, a in ffn_phases(base, 0):
                    if kind == "up":
                        phase(u0, n, lambda f: up[f + a])
                    else:
                        phase(u0, n, lambda m: down[0 if a == 0 else 1][m])

            ffn(0, up1, down1)
            load(U_MIX, 0, w_ga)
            phase(U_MIX + 1, 8, lambda n: w_proj[n])
            phase(U_MIX + 9, 4, lambda n: w_v[n])
            phase(U_MIX + 13, 4, lambda n: w_o[n])
            ffn(U_FFN2, up2, down2)
            for m in range(KC):
                sp.wait_ge(fin_done, m + 1)
                sp.dma_start(outT[m], x[:, m, :]).then_inc(stored, 16)
            sp.wait_ge(stored, 16 * KC)

        @block.gpsimd
        def _(pool):
            count = [0]

            def step(ins):
                count[0] += 1
                ins.then_inc(pool_step, 1)
                pool.wait_ge(pool_step, count[0])

            pool.wait_ge(pos_landed, 16)
            pool.wait_ge(const_landed, 16 * 3)
            step(nc.gpsimd.tensor_copy(ang[:], pos_i[:]))
            step(nc.gpsimd.tensor_scalar(ang[:], ang[:], const[:, C_FREQ:C_FREQ + 1], None, ALU.mult))
            for table, quarter in ((rope_s, 0.0), (rope_c, 0.25)):
                step(nc.gpsimd.tensor_scalar(turn[:], ang[:], 1 / (2 * math.pi), quarter, ALU.mult, ALU.add))
                step(nc.gpsimd.tensor_scalar(turn[:], turn[:], MAGIC, None, ALU.add))
                step(nc.gpsimd.tensor_scalar(turn[:], turn[:], -MAGIC, None, ALU.add))
                left = ang
                for c in TWO_PI:
                    step(nc.gpsimd.tensor_scalar(part[:], turn[:], c, None, ALU.mult))
                    step(nc.gpsimd.tensor_tensor(table[:], left[:], part[:], ALU.subtract))
                    left = table
                if quarter:
                    step(nc.gpsimd.tensor_scalar(table[:], table[:], math.pi / 2, None, ALU.add))
                last = nc.gpsimd.tensor_scalar(table[:], table[:], 3.1415925, -3.1415925, ALU.min, ALU.max)
                last.then_inc(ang_sin, 1)
            for n in range(2 * ST):
                t = T_AQ + n // 2 if n % 2 == 0 else T_AK + n // 2
                pool.wait_ge(rope_tab, 2)
                pool.wait_ge(rope_shuf, n + 1)
                nc.gpsimd.tensor_tensor(projT[:, t, :], projT[:, t, :], rope_c[:], ALU.mult).then_inc(rope_cos, 1)

        @block.scalar
        def _(act):
            def split(u, i, size):
                act.wait_ge(w_in[u % 2], 16 * (u // 2 + 1) + 16 * i)
                nc.scalar.activation(w_hi[u % 2][:, 0:size], raw[u % 2][:, 0:size], ACT.Copy).then_inc(w_round, 1)

            def split_next(u, i, tiles):
                if isinstance(i, int):
                    u, i = u + 2 * i, 0
                if u + 2 < N_UNITS:
                    act.wait_ge(tile_done, tiles)
                    split(u + 2, i, unit_size(u + 2))

            def round_h(layer, m, col):
                nc.scalar.activation(h_hi[:, m, :], x[:, m, :], ACT.Copy,
                                     scale=gains[:, col + m, :]).then_inc(h_round, 1)

            def square_x(layer, m):
                act.wait_ge(sq_added, 9 * layer + 1 + m)
                act.nop(nofuse=True)
                nc.scalar.activation(square[:], x[:, m, :], ACT.Square).then_inc(sq_done, 1)

            def root(n):
                act.wait_ge(sums_out, n + 1)
                nc.scalar.activation(rstd[:], rstd[:], ACT.Sqrt).then_inc(root_done, 1)

            def ffn(layer, base, tbase, g_hi, gate, prod, next_gain):
                gb = FT * (layer // 2)
                for kind, u0, t0, n, a in ffn_phases(base, tbase):
                    def up(i, j):
                        f = 2 * i + j
                        t = t0 + 2 * f
                        act.wait_ge(tile_out, BANK_CREDIT + t + 1)
                        nc.scalar.activation(gate[:], gate[:], ACT.Silu).then_inc(silu_done, 1)
                        split_next(u0 + j, i, t + 2)
                        act.wait_ge(g_mul, gb + a + f + 1)
                        nc.scalar.activation(g_hi[:, f, :], prod[:], ACT.Copy).then_inc(g_round, 1)

                    def down(i, j):
                        m = 2 * i + j
                        if a:
                            act.wait_ge(tile_out, BANK_CREDIT + t0 + m + 1)
                            if layer == 0:
                                round_h(1, m, next_gain)
                            square_x(layer + 1, m)
                        split_next(u0 + j, i, t0 + m + 1)

                    step = up if kind == "up" else down
                    if kind == "up" and a == 0:
                        root(NORM[layer])
                    with act.Fori(0, n // 2 - 1) as i:
                        for j in range(2):
                            step(i, j)
                    for j in range(2):
                        step(n // 2 - 1, j)

            act.dma_start(x[:, 0:4, :], xT_in[0:4].rearrange("c p s -> p c s")).then_inc(x_in[0], 16)
            act.dma_start(const[:], const_in).then_inc(const_landed, 16)
            act.dma_start(gains[:].rearrange("p n a -> p (n a)"), gains_in).then_inc(const_landed, 16)
            act.dma_start(x[:, 4:8, :], xT_in[4:8].rearrange("c p s -> p c s")).then_inc(x_in[1], 16)
            act.dma_start(wa2[:], w_a2).then_inc(const_landed, 16)
            act.dma_start(pos_i[:], positions.partition_broadcast(P)).then_inc(pos_landed, 16)
            act.wait_ge(const_landed, 48)
            split(0, 0, unit_size(0))
            for m in range(KC):
                act.wait_ge(x_in[m // 4], 16)
                round_h(0, m, G_FFN1)
                square_x(0, m)
            split(1, 0, unit_size(1))
            ffn(0, 0, 0, ffn_mem[1][0], ffn_mem[1][2], ffn_mem[1][3], G_MIX)

            act.wait_ge(ang_sin, 2)
            nc.scalar.activation(rope_s[:], rope_s[:], ACT.Sin).then_inc(rope_tab, 1)
            nc.scalar.activation(rope_c[:], rope_c[:], ACT.Sin).then_inc(rope_tab, 1)
            root(1)
            act.wait_ge(sums_out, 3)
            nc.scalar.activation(rstd_tok[:], rstd_tok[:], ACT.Sqrt).then_inc(root_done, 1)
            split_next(U_MIX, 0, T_MIX + 1)
            UA, TA = U_MIX + 1, T_MIX + 1
            with act.Fori(0, 3) as i:
                for j in range(2):
                    split_next(UA + j, i, TA + 4 * i + 2 * j + 2)
            for j in range(2):
                split_next(UA + j, 3, TA + 12 + 2 * j + 2)
            for n in range(4):
                act.wait_ge(tile_out, BANK_CREDIT + TA + 16)
                nc.scalar.activation(projT[:, T_GR + n, :], projT[:, T_GR + n, :], ACT.Silu).then_inc(gr_done, 1)
            for p in range(2):
                act.wait_ge(z_done, p + 1)
                nc.scalar.activation(gt[0][p][:], ps[4 + p][:], ACT.Identity,
                                     bias=gains[:, G_BA + p, :]).then_inc(z_out, 1)
            for p in range(2):
                act.wait_ge(z_out, p + 1)
                nc.scalar.activation(gt[1][p][:], gt[0][p][:], ACT.Abs).then_inc(act_step, 1)
            for p in range(2):
                act.wait_ge(act_step, p + 1)
                nc.scalar.activation(gt[1][p][:], gt[1][p][:], ACT.Exp, scale=-1.0).then_inc(act_step, 1)
            UV, TV = UA + 8, TA + 16
            act.wait_ge(v_half, 1)
            split(UV + 2, 0, unit_size(UV + 2))
            for p in range(2):
                act.wait_ge(act_step, p + 3)
                nc.scalar.activation(gt[1][p][:], gt[1][p][:], ACT.Ln, bias=ones[:, 0:1]).then_inc(log_done, 1)
            split_next(UV + 1, 0, TV + 4)
            act.wait_ge(v_half, 2)
            split(UV + 4, 0, unit_size(UV + 4))
            split_next(UV + 3, 0, TV + 8)

            def exp_scores(q):
                h, i = q // 4, q % 4
                off = P * i * (i + 1) // 2
                strip = probs[h % 2][:, off:off + P * (i + 1)]
                act.wait_ge(negm_done, q + 1)
                nc.scalar.activation(strip, strip, ACT.Exp, bias=negm[:, q:q + 1],
                                     accum_out=den[:, q:q + 1]).then_inc(exp_done, 1)

            def move_probsT(h, i):
                act.wait_ge(pt_done, 4 * h + i + 1)
                if h >= 2:
                    act.wait_ge(o_done, h - 1)
                nc.scalar.activation(probsT[h % 2][:, 0:i + 1, i * P:(i + 1) * P],
                                     ps[2 + i][:, 0:(i + 1) * P].rearrange("p (j q) -> p j q", q=P),
                                     ACT.Copy).then_inc(pt_out, 1)

            def gla_exps(p):
                act.wait_ge(b_done, p + 1)
                nc.scalar.activation(gt[0][p][:], gt[1][p][:], ACT.Exp, scale=1 / 16).then_inc(eb_done, 1)
                nc.scalar.activation(gt[2][p][:], gt[1][p][:], ACT.Exp, scale=-1 / 16).then_inc(eb_done, 1)

            def gla_tail(p):
                act.wait_ge(tail_done, p + 1)
                nc.scalar.activation(gt[1][p][:], rope_c[:], ACT.Exp, scale=1 / 16).then_inc(et_done, 1)

            for i in range(4):
                exp_scores(i)
            for h in range(ATT_H):
                for i in range(4):
                    if h + 1 < ATT_H:
                        exp_scores(4 * (h + 1) + i)
                    move_probsT(h, i)
                if h in (1, 3):
                    gla_exps(h // 2)
                if h in (2, 4):
                    gla_tail(h // 2 - 1)
            for p in range(2):
                act.wait_ge(ktail_done, p + 1)
                nc.scalar.activation(k_tok[p][:].rearrange("p t c -> p (t c)"), ps[p][:], ACT.Copy).then_inc(ktail_out, 1)
            root(3)
            for k in range(4):
                act.wait_ge(att_scaled, k + 1)
                nc.scalar.activation(h_hi[:, 4 + k, :], projT[:, T_AQ + k, :], ACT.Copy).then_inc(h_round, 1)
            for g in range(GLA_H):
                act.wait_ge(sums_out, 5 + g)
                nc.scalar.activation(head_rstd[g % 2][:], head_rstd[g % 2][:], ACT.Sqrt).then_inc(root_done, 1)
                act.wait_ge(gla_scaled, g + 1)
                nc.scalar.activation(h_hi[:, g, :], projT[:, T_AK + g, :], ACT.Copy).then_inc(h_round, 1)
            UO, TO = UV + 4, TV + 8
            for n in range(4):
                for w in range(2):
                    m = 2 * n + w
                    act.wait_ge(tile_out, BANK_CREDIT + TO + m + 1)
                    square_x(2, m)
                split_next(UO + n, 0, TO + 2 * n + 2)
            for m in range(KC):
                act.wait_ge(tile_done, TO + 8)
                round_h(2, m, G_FFN2)
            ffn(2, U_FFN2, T_FFN2, ffn_mem[2][0], ffn_mem[2][2], ffn_mem[2][3], None)
            root(9)

        @block.vector
        def _(dve):
            def split(u, i, size):
                dve.wait_ge(w_round, u + 1 + 2 * i)
                nc.vector.tensor_tensor(w_lo[u % 2][:, 0:size], raw[u % 2][:, 0:size],
                                        w_hi[u % 2][:, 0:size].bitcast(F32), ALU.subtract).then_inc(w_split, 1)

            def split_next(u, i):
                if isinstance(i, int):
                    u, i = u + 2 * i, 0
                if u + 2 < N_UNITS:
                    split(u + 2, i, unit_size(u + 2))

            def low_h(count, m, col):
                dve.wait_ge(h_round, count + 1)
                nc.vector.scalar_tensor_tensor(h_lo[:, m, :], x[:, m, :], gains[:, col + m, :],
                                               h_hi[:, m, :].bitcast(F32), ALU.mult, ALU.subtract).then_inc(h_ready, 1)

            def clear_sums():
                nc.vector.memset(sumsq[:], 0.0).then_inc(sq_added, 1)

            def add_square(layer, m):
                dve.wait_ge(sq_done, 8 * layer + m + 1)
                dve.wait_ge(sq_added, 9 * layer + m + 1)
                nc.vector.tensor_tensor(sumsq[:], sumsq[:], square[:], ALU.add).then_inc(sq_added, 1)

            def mean_square(n, bank, width, out):
                dve.wait_ge(sums_done, n + 1)
                nc.vector.tensor_scalar(out, bank, 1.0 / width, EPS, ALU.mult, ALU.add).then_inc(sums_out, 1)

            def reciprocal_root(n, out):
                dve.wait_ge(root_done, n + 1)
                nc.vector.reciprocal(out, out).then_inc(rstd_done, 1)
                dve.wait_ge(rstd_done, n + 1)

            def ffn(layer, base, tbase, g_hi, g_lo, gate, prod, next_gain):
                gb = FT * (layer // 2)
                for kind, u0, t0, n, a in ffn_phases(base, tbase):
                    def up(i, j):
                        f = 2 * i + j
                        t = t0 + 2 * f
                        dve.wait_ge(tile_done, t + 1)
                        nc.vector.tensor_tensor(gate[:], ps[2 * j][:], rstd[:], ALU.mult).then_inc(tile_out, 1)
                        dve.wait_ge(tile_done, t + 2)
                        nc.vector.tensor_tensor(prod[:], ps[2 * j + 1][:], rstd[:], ALU.mult).then_inc(tile_out, 1)
                        dve.wait_ge(silu_done, gb + a + f + 1)
                        dve.wait_ge(tile_out, BANK_CREDIT + t + 2)
                        nc.vector.tensor_tensor(prod[:], prod[:], gate[:], ALU.mult).then_inc(g_mul, 1)
                        split_next(u0 + j, i)
                        dve.wait_ge(g_round, gb + a + f + 1)
                        nc.vector.tensor_tensor(g_lo[:, f, :], prod[:], g_hi[:, f, :].bitcast(F32),
                                                ALU.subtract).then_inc(g_ready, 1)
                        dve.wait_ge(g_ready, gb + a + f + 1)

                    def down(i, j):
                        m = 2 * i + j
                        dve.wait_ge(tile_done, t0 + m + 1)
                        nc.vector.scalar_tensor_tensor(x[:, m, :], ps[4 + j][:], 0.5, x[:, m, :],
                                                       ALU.mult, ALU.add).then_inc(tile_out, 1)
                        if a:
                            if layer == 0:
                                low_h(8 + m, m, next_gain)
                            add_square(layer + 1, m)
                        split_next(u0 + j, i)

                    step = up if kind == "up" else down
                    if kind == "up" and a == 0:
                        mean_square(NORM[layer], ps[6][:], D, rstd[:])
                        reciprocal_root(NORM[layer], rstd[:])
                        clear_sums()
                    with dve.Fori(0, n // 2 - 1) as i:
                        for j in range(2):
                            step(i, j)
                    for j in range(2):
                        step(n // 2 - 1, j)

            nc.vector.memset(credit[:], 0.0).then_inc(tile_out, BANK_CREDIT)
            clear_sums()
            split(0, 0, unit_size(0))
            for m in range(KC):
                low_h(m, m, G_FFN1)
                add_square(0, m)
            split(1, 0, unit_size(1))
            ffn(0, 0, 0, *ffn_mem[1], G_MIX)

            steps = [0]

            def chain(ins):
                steps[0] += 1
                ins.then_inc(dve_step, 1)
                dve.wait_ge(dve_step, steps[0])

            mean_square(1, ps[6][:], D, rstd[:])
            mean_square(2, ps[7][:, 0:ST], D, rstd_tok[:])
            reciprocal_root(1, rstd[:])
            reciprocal_root(2, rstd_tok[:])
            clear_sums()
            UA, TA = U_MIX + 1, T_MIX + 1
            dve.wait_ge(tile_done, T_MIX + 1)
            nc.vector.tensor_tensor(projT[:, T_GA, :], ps[4][:], rstd[:], ALU.mult).then_inc(tile_out, 1)
            split_next(U_MIX, 0)

            def project(i, j):
                for w in range(2):
                    k = 4 * i + 2 * j + w
                    dve.wait_ge(tile_done, TA + k + 1)
                    nc.vector.tensor_tensor(projT[:, k, :], ps[2 * j + w][:], rstd[:], ALU.mult).then_inc(tile_out, 1)
                split_next(UA + j, i)

            with dve.Fori(0, 3) as i:
                for j in range(2):
                    project(i, j)
            for j in range(2):
                project(3, j)

            def rotate(n):
                t = T_AQ + n // 2 if n % 2 == 0 else T_AK + n // 2
                if n == 0:
                    dve.wait_ge(rope_tab, 1)
                    chain(nc.vector.tensor_scalar(rope_s[:], rope_s[:], const[:, C_SGN:C_SGN + 1], None, ALU.mult))
                if n:
                    dve.wait_ge(rope_done, n)
                half = ROT // 2
                nc.vector.stream_shuffle(square[:], projT[:, t, :],
                                         [(c + half) % ROT if c < ROT else c for c in range(32)]).then_inc(rope_shuf, 1)
                dve.wait_ge(rope_shuf, n + 1)
                nc.vector.tensor_tensor(square[:], square[:], rope_s[:], ALU.mult).then_inc(rope_sin, 1)
                dve.wait_ge(rope_sin, n + 1)
                dve.wait_ge(rope_cos, n + 1)
                nc.vector.tensor_tensor(projT[:, t, :], projT[:, t, :], square[:], ALU.add).then_inc(rope_done, 1)

            UV, TV = UA + 8, TA + 16
            split(UV + 2, 0, unit_size(UV + 2))
            rotate(0)
            rotate(1)
            for s, values in enumerate((v_att, v_gla)):
                rotate(4 * s + 2)
                rotate(4 * s + 3)
                for t in range(ST):
                    dve.wait_ge(tile_done, TV + 4 * s + t + 1)
                    nc.vector.tensor_scalar(values[:, t, :], ps[4 * s + t][:], rstd_tok[:, t:t + 1], None,
                                            ALU.mult).then_inc(tile_out, 1)
                split(UV + 2 * s + 3, 0, unit_size(UV + 2 * s + 3))
                if s == 0:
                    rotate(4)
                    rotate(5)
                    split(UV + 4, 0, unit_size(UV + 4))

            def mask_scores(q):
                h, i = q // 4, q % 4
                off, width = P * i * (i + 1) // 2, P * (i + 1)
                dve.wait_ge(s_done, q + 1)
                if h >= 2:
                    dve.wait_ge(pt_done, 4 * (h - 2) + i + 1)
                nc.vector.tensor_tensor_reduce(out=probs[h % 2][:, off:off + width], in0=ps[i % 2][:, 0:width],
                                               in1=const[:, C_STRIP + S - width:C_STRIP + S],
                                               scale=SCORE_SCALE, scalar=-3e38, op0=ALU.add, op1=ALU.max,
                                               accum_out=mx[:, q:q + 1]).then_inc(s_masked, 1)
                dve.wait_ge(s_masked, q + 1)
                nc.vector.tensor_scalar(negm[:, q:q + 1], mx[:, q:q + 1], -1.0, None, ALU.mult).then_inc(negm_done, 1)

            def scaled_identity(q):
                dve.wait_ge(exp_done, q + 1)
                nc.vector.reciprocal(rden[:, q:q + 1], den[:, q:q + 1]).then_inc(rden_done, 1)
                dve.wait_ge(rden_done, q + 1)
                if q >= NDIAG:
                    dve.wait_ge(pt_done, q - NDIAG + 1)
                nc.vector.tensor_scalar(diag[:, q % NDIAG, :], ident, rden[:, q:q + 1], None,
                                        ALU.mult).then_inc(diag_done, 1)

            def move_out(h):
                r = HD * (h % 2)
                dve.wait_ge(o_done, h + 1)
                nc.vector.tensor_copy(projT[r:r + HD, T_AQ + h // 2, :], ps[6 + h % 2][r:r + HD, :]).then_inc(o_out, 1)

            def gla_cumsum(p):
                dve.wait_ge(log_done, p + 1)
                chain(nc.vector.scalar_tensor_tensor(gt[0][p][:], gt[0][p][:], 0.0, gt[1][p][:], ALU.min, ALU.subtract))
                nc.vector.tensor_tensor_scan(gt[1][p][:], const[:, C_SCAN:C_SCAN + S], gt[0][p][:], 0.0,
                                             ALU.mult, ALU.add).then_inc(b_done, 1)

            def gla_decay(p):
                dve.wait_ge(b_done, p + 1)
                if p:
                    dve.wait_ge(et_done, p)
                b = gt[1][p][:].rearrange("p (c t) -> p c t", t=CHUNK)
                nc.vector.tensor_tensor(rope_c[:].rearrange("p (c t) -> p c t", t=CHUNK),
                                        b[:, :, CHUNK - 1:CHUNK].broadcast_to([P, NCH, CHUNK]), b,
                                        ALU.subtract).then_inc(tail_done, 1)

            def gla_scale(p):
                dve.wait_ge(et_done, p + 1)
                nc.vector.tensor_tensor(gt[1][p][:], projT[:, T_GK + p, :], gt[1][p][:], ALU.mult).then_inc(gla_ready, 1)
                nc.vector.tensor_tensor(projT[:, T_GK + p, :], projT[:, T_GK + p, :], gt[2][p][:],
                                        ALU.mult).then_inc(gla_ready, 1)
                nc.vector.scalar_tensor_tensor(projT[:, T_GQ + p, :], projT[:, T_GQ + p, :], GLA_DK ** -0.5,
                                               gt[0][p][:], ALU.mult, ALU.mult).then_inc(gla_ready, 1)

            for q in range(4):
                mask_scores(q)
                if q:
                    scaled_identity(q - 1)
            for h in range(ATT_H):
                for i in range(4):
                    q = 4 * (h + 1) + i
                    if h + 1 < ATT_H:
                        mask_scores(q)
                        scaled_identity(q - 1)
                if h + 1 == ATT_H:
                    scaled_identity(4 * ATT_H - 1)
                if h:
                    move_out(h - 1)
                if h in (1, 3):
                    gla_cumsum(h // 2)
                if h in (2, 4):
                    gla_decay(h // 2 - 1)
                if h in (3, 5):
                    gla_scale(h // 2 - 1)
            move_out(ATT_H - 1)
            dve.wait_ge(o_out, ATT_H)
            dve.wait_ge(et_done, 2)
            for k in range(4):
                o = projT[:, T_AQ + k, :]
                if k == 0:
                    chain(nc.vector.tensor_tensor(rope_s[:], o, o, ALU.mult))
                else:
                    chain(nc.vector.tensor_tensor(square[:], o, o, ALU.mult))
                    nc.vector.tensor_tensor(rope_s[:], rope_s[:], square[:], ALU.add).then_inc(att_squares, 1)
                    dve.wait_ge(att_squares, k)
            dve.wait_ge(pt_done, 4 * ATT_H)
            dve.wait_ge(o_done, ATT_H)
            for j in range(2):
                nc.vector.memset(att_g[j][:], 0.0).then_inc(dve_step, 1)
                steps[0] += 1
            dve.wait_ge(dve_step, steps[0])

            tri = const[:, C_TRI:C_TRI + S].bitcast(U32)
            for g in range(GLA_H):
                dve.wait_ge(ag_done, g + 1)
                if g >= 2:
                    dve.wait_ge(og_done, g - 1)
                nc.vector.copy_predicated(att_g[g % 2][:], tri, ps[2 + g][:]).then_inc(ag_out, 1)
                if g == 1:
                    dve.wait_ge(u_done, 2 * (NCH - 1))
                    for c in range(NCH - 1):
                        for p in range(2):
                            u = ps[6 + c % 2 if p == 0 else c % 2][:, (c // 2) * P:(c // 2 + 1) * P]
                            if c == 0:
                                ins = nc.vector.tensor_copy(state[p][:, 1, :], u)
                            else:
                                dve.wait_ge(state_done, 2 * c + p - 1)
                                ins = nc.vector.scalar_tensor_tensor(
                                    state[p][:, c + 1, :], state[p][:, c, :],
                                    gt[0][p][:, c * CHUNK + CHUNK - 1:c * CHUNK + CHUNK], u, ALU.mult, ALU.add)
                            ins.then_inc(state_done, 1)
            mean_square(3, ps[6][:], ATT_W, rstd[:])
            reciprocal_root(3, rstd[:])
            for k in range(4):
                nc.vector.scalar_tensor_tensor(projT[:, T_AQ + k, :], projT[:, T_AQ + k, :],
                                               gains[:, G_ATT + k, :], rstd[:],
                                               ALU.mult, ALU.mult).then_inc(att_scaled, 1)
            for k in range(4):
                dve.wait_ge(h_round, 16 + k + 1)
                nc.vector.tensor_tensor(h_lo[:, 4 + k, :], projT[:, T_AQ + k, :], h_hi[:, 4 + k, :].bitcast(F32),
                                        ALU.subtract).then_inc(h_ready, 1)
            for g in range(GLA_H):
                dve.wait_ge(og_done, g + 1)
                o = projT[:, T_AK + g, :]
                nc.vector.tensor_copy(o, ps[2 + g][:]).then_inc(og_out, 1)
                dve.wait_ge(og_out, 2 * g + 1)
                if g:
                    dve.wait_ge(sums_done, 4 + g)
                nc.vector.tensor_tensor(square[:], o, o, ALU.mult).then_inc(og_out, 1)
                mean_square(4 + g, ps[7 - 7 * (g % 2)][:], GLA_DV, head_rstd[g % 2][:])
                reciprocal_root(4 + g, head_rstd[g % 2][:])
                chain(nc.vector.tensor_tensor(o, o, head_rstd[g % 2][:], ALU.mult))
                dve.wait_ge(gr_done, g + 1)
                nc.vector.scalar_tensor_tensor(o, o, gains[:, G_GLA + g, :], projT[:, T_GR + g, :],
                                               ALU.mult, ALU.mult).then_inc(gla_scaled, 1)
                dve.wait_ge(h_round, 20 + g + 1)
                nc.vector.tensor_tensor(h_lo[:, g, :], o, h_hi[:, g, :].bitcast(F32), ALU.subtract).then_inc(h_ready, 1)
            UO, TO = UV + 4, TV + 8
            for n in range(4):
                for w in range(2):
                    m = 2 * n + w
                    dve.wait_ge(tile_done, TO + m + 1)
                    nc.vector.tensor_tensor(x[:, m, :], x[:, m, :], ps[OUT_BANKS[m % 4]][:], ALU.add).then_inc(tile_out, 1)
                    add_square(2, m)
                split_next(UO + n, 0)
            for m in range(KC):
                low_h(24 + m, m, G_FFN2)
            ffn(2, U_FFN2, T_FFN2, *ffn_mem[2], None)
            mean_square(9, ps[6][:], D, rstd[:])
            reciprocal_root(9, rstd[:])
            for m in range(KC):
                nc.vector.scalar_tensor_tensor(x[:, m, :], x[:, m, :], gains[:, G_FINAL + m, :], rstd[:],
                                               ALU.mult, ALU.mult).then_inc(fin_done, 1)

        @block.tensor
        def _(pe):
            def product(out, a_hi, a_lo, b_hi, b_lo, first, last):
                nc.tensor.matmul(out, a_hi, b_hi, start=first, stop=False)
                nc.tensor.matmul(out, a_hi, b_lo, start=False, stop=False)
                return nc.tensor.matmul(out, a_lo, b_hi, start=False, stop=last)

            def tile_of(slot, w, bank, order=range(KC), wait=None, base=0, hidden_g=None):
                m_hi, m_lo = hidden_g or (h_hi, h_lo)
                for pos, k in enumerate(order):
                    if wait is not None:
                        pe.wait_ge(wait, base + pos + 1)
                    col = (w * KC + k) * P if hidden_g is None else k * P
                    last = product(ps[bank][:], w_hi[slot][:, col:col + P], w_lo[slot][:, col:col + P],
                                   m_hi[:, k, :], m_lo[:, k, :], pos == 0, pos == len(order) - 1)
                last.then_inc(tile_done, 1)

            def channel_sums(n, bank, squares):
                nc.tensor.matmul(ps[bank][:], ones, squares, start=True, stop=True).then_inc(sums_done, 1)

            def ffn(layer, base, tbase, g_hi, g_lo, gate, prod):
                gb = FT * (layer // 2)
                for kind, u0, t0, n, a in ffn_phases(base, tbase):
                    def up(i, j, first=False):
                        pe.wait_ge(w_split, u0 + j + 1 + 2 * i)
                        for w in range(2):
                            t = t0 + 4 * i + 2 * j + w
                            pe.wait_ge(tile_out, t + BANK_CREDIT - 3)
                            tile_of((u0 + j) % 2, w, 2 * j + w, wait=h_ready if first and w == 0 else None,
                                    base=12 * layer)
                        if first:
                            pe.wait_ge(sq_added, 9 * layer + 9)
                            if layer:
                                pe.wait_ge(tile_out, BANK_CREDIT + t0)
                            channel_sums(NORM[layer], 6, sumsq[:])

                    def down(i, j, first=False):
                        t = t0 + 2 * i + j
                        pe.wait_ge(w_split, u0 + j + 1 + 2 * i)
                        pe.wait_ge(tile_out, t + BANK_CREDIT - 1)
                        tile_of((u0 + j) % 2, 0, 4 + j, order=range(parts[a]), wait=g_ready if first else None,
                                base=gb + a, hidden_g=(g_hi, g_lo))

                    step = up if kind == "up" else down
                    step(0, 0, first=kind == "down" or a == 0)
                    step(0, 1)
                    with pe.Fori(1, n // 2) as i:
                        for j in range(2):
                            step(i, j)

            parts = {a: b - a for a, b in PARTS}
            pe.wait_ge(const_landed, 48)
            ffn(0, 0, 0, *ffn_mem[1])

            pe.wait_ge(w_split, U_MIX + 1)
            pe.wait_ge(tile_out, BANK_CREDIT + T_MIX - 1)
            tile_of(U_MIX % 2, 0, 4, wait=h_ready, base=8)
            pe.wait_ge(sq_added, 18)
            channel_sums(1, 6, sumsq[:])
            for t in range(ST):
                last = nc.tensor.matmul(ps[7][:, t:t + 1], sumsq[:, t * P:(t + 1) * P], ones[:, 0:1],
                                        start=True, stop=True)
            last.then_inc(sums_done, 1)
            UA, TA = U_MIX + 1, T_MIX + 1
            with pe.Fori(0, 4) as i:
                for j in range(2):
                    pe.wait_ge(w_split, UA + j + 1 + 2 * i)
                    for w in range(2):
                        pe.wait_ge(tile_out, TA + 4 * i + 2 * j + w + BANK_CREDIT - 3)
                        tile_of((UA + j) % 2, w, 2 * j + w)
            pe.wait_ge(tile_out, BANK_CREDIT + T_MIX + 1)
            for p in range(2):
                nc.tensor.matmul(ps[4 + p][:], wa2[:, p * P:(p + 1) * P], projT[0:GLA_RANK, T_GA, :],
                                 start=True, stop=True).then_inc(z_done, 1)
            UV, TV = UA + 8, TA + 16
            for s in range(2):
                for half in range(2):
                    slot = (UV + 2 * s + half) % 2
                    pe.wait_ge(w_split, UV + 2 * s + half + 1)
                    for t in range(ST):
                        bank = 4 * s + t
                        if half == 0 and s == 0:
                            pe.wait_ge(tile_out, BANK_CREDIT + TA + 12 + t + 1)
                        if half == 0 and s == 1:
                            if bank < 6:
                                pe.wait_ge(z_out, bank - 3)
                            else:
                                pe.wait_ge(sums_out, bank - 4)
                        for k in range(4):
                            c = 4 * half + k
                            tok = slice(t * P, (t + 1) * P)
                            cols = slice(k * S, (k + 1) * S)
                            last = product(ps[bank][:], h_hi[:, c, tok], h_lo[:, c, tok],
                                           w_hi[slot][:, cols], w_lo[slot][:, cols], c == 0, c == KC - 1)
                        if half:
                            last.then_inc(tile_done, 1)
                    if half == 0:
                        last.then_inc(v_half, 1)

            def scores(h, i):
                q = 4 * h + i
                r = HD * (h % 2)
                if i == 0:
                    pe.wait_ge(rope_done, 2 * (h // 2) + 2)
                if q >= 2:
                    pe.wait_ge(s_masked, q - 1)
                else:
                    pe.wait_ge(tile_out, BANK_CREDIT + TV + 4)
                nc.tensor.matmul(ps[i % 2][:, 0:(i + 1) * P], projT[r:r + HD, T_AQ + h // 2, i * P:(i + 1) * P],
                                 projT[r:r + HD, T_AK + h // 2, 0:(i + 1) * P], start=True, stop=True).then_inc(s_done, 1)

            def transpose_probs(h, i):
                q = 4 * h + i
                off = P * i * (i + 1) // 2
                pe.wait_ge(diag_done, q + 1)
                if h:
                    pe.wait_ge(pt_out, q - 3)
                else:
                    pe.wait_ge(tile_out, BANK_CREDIT + TV + 8)
                for j in range(i + 1):
                    last = nc.tensor.matmul(ps[2 + i][:, j * P:(j + 1) * P], probs[h % 2][:, off + j * P:off + (j + 1) * P],
                                            diag[:, q % NDIAG, :], start=True, stop=True)
                last.then_inc(pt_done, 1)

            def weigh_values(h):
                r = HD * (h % 2)
                pe.wait_ge(pt_out, 4 * h + 4)
                if h >= 2:
                    pe.wait_ge(o_out, h - 1)
                for j in range(ST):
                    last = nc.tensor.matmul(ps[6 + h % 2][r:r + HD, j * P:S], v_att[:, j, h * HD:(h + 1) * HD],
                                            probsT[h % 2][:, j, j * P:S], start=j == 0, stop=j == ST - 1)
                last.then_inc(o_done, 1)

            for i in range(4):
                scores(0, i)
            for h in range(ATT_H):
                for i in range(4):
                    if h + 1 < ATT_H:
                        scores(h + 1, i)
                    transpose_probs(h, i)
                    if i == 1 and h:
                        weigh_values(h - 1)
            weigh_values(ATT_H - 1)

            for p in range(2):
                pe.wait_ge(gla_ready, 3 * p + 1)
                for t in range(ST):
                    last = nc.tensor.transpose(ps[p][:, t * P:(t + 1) * P], gt[1][p][:, t * P:(t + 1) * P], ident)
                last.then_inc(ktail_done, 1)
            for g in range(GLA_H):
                p, r = g // 2, GLA_DK * (g % 2)
                pe.wait_ge(gla_ready, 3 * p + 3)
                pe.wait_ge(pt_out, 4 * ATT_H)
                for t in range(ST):
                    tok = slice(t * P, (t + 1) * P)
                    last = nc.tensor.matmul(ps[2 + g][:, tok], projT[r:r + GLA_DK, T_GK + p, tok],
                                            projT[r:r + GLA_DK, T_GQ + p, tok], start=True, stop=True)
                last.then_inc(ag_done, 1)
            pe.wait_ge(o_out, ATT_H)
            pe.wait_ge(ktail_out, 2)
            for c in range(NCH - 1):
                rows = slice(CHUNK * (c % 2), CHUNK * (c % 2) + CHUNK)
                for p in range(2):
                    bank = 6 + c % 2 if p == 0 else c % 2
                    for hh in range(2):
                        g = 2 * p + hh
                        last = nc.tensor.matmul(ps[bank][hh * GLA_DK:(hh + 1) * GLA_DK, (c // 2) * P:(c // 2 + 1) * P],
                                                k_tok[p][rows, c // 2, hh * GLA_DK:(hh + 1) * GLA_DK],
                                                v_gla[rows, c // 2, g * P:(g + 1) * P], start=True, stop=True)
                    last.then_inc(u_done, 1)

            def gla_output(g):
                p, r = g // 2, GLA_DK * (g % 2)
                pe.wait_ge(ag_out, g + 1)
                for t in range(ST):
                    tok = slice(t * P, (t + 1) * P)
                    nc.tensor.matmul(ps[2 + g][:, tok], v_gla[:, t, g * P:(g + 1) * P], att_g[g % 2][:, tok],
                                     start=t == 0, stop=False, skip_group_check=True)
                for c in range(1, NCH):
                    pe.wait_ge(state_done, 2 * (c - 1) + p + 1)
                    tok = slice(c * CHUNK, (c + 1) * CHUNK)
                    last = nc.tensor.matmul(ps[2 + g][:, tok], state[p][r:r + GLA_DK, c, :],
                                            projT[r:r + GLA_DK, T_GQ + p, tok],
                                            start=False, stop=c == NCH - 1, skip_group_check=True)
                last.then_inc(og_done, 1)

            def gla_sums(g):
                pe.wait_ge(og_out, 2 * g + 2)
                if g >= 2:
                    pe.wait_ge(sums_out, 3 + g)
                channel_sums(4 + g, 7 - 7 * (g % 2), square[:])

            gla_output(0)
            pe.wait_ge(state_done, 2 * (NCH - 1))
            pe.wait_ge(att_squares, 3)
            channel_sums(3, 6, rope_s[:])
            for g in range(1, GLA_H):
                gla_output(g)
            for g in range(GLA_H):
                gla_sums(g)

            UO, TO = UV + 4, TV + 8
            for n in range(4):
                pe.wait_ge(w_split, UO + n + 1)
                for w in range(2):
                    m = 2 * n + w
                    if m == 0:
                        pe.wait_ge(sums_out, 4)
                    elif m >= 4:
                        pe.wait_ge(tile_out, BANK_CREDIT + TO + m - 3)
                    tile_of((UO + n) % 2, w, OUT_BANKS[m % 4], order=(4, 5, 6, 7, 0, 1, 2, 3),
                            wait=h_ready if m == 0 else None, base=16)
            ffn(2, U_FFN2, T_FFN2, *ffn_mem[2])
            pe.wait_ge(sq_added, 36)
            channel_sums(9, 6, sumsq[:])


def _constants():
    c = np.zeros((P, N_CONST), np.float32)
    row = np.arange(P)
    c[:, C_ID:C_ID + P] = np.eye(P)
    c[:, C_ONE:C_ONE + P] = 1.0
    dist = (S - P + row)[:, None] - np.arange(S)[None, :]
    seen = sum(((dist >= 0) & (dist % d == 0) & (dist // d <= w // d)).astype(np.float64) for w, d in PATTERNS)
    c[:, C_STRIP:C_STRIP + S] = np.where(seen > 0, np.log(np.maximum(seen, 1)) / SCORE_SCALE, FAR)
    tri = (row[:, None] // CHUNK == row[None, :] // CHUNK) & (row[:, None] <= row[None, :])
    c[:, C_TRI:C_TRI + S] = np.tile(tri, (1, ST))
    c[:, C_SCAN:C_SCAN + S] = (np.arange(S) % CHUNK != 0)[None, :]
    dim = row % HD
    freq = np.float32(THETA) ** (-np.arange(0, ROT, 2, dtype=np.float32) / np.float32(ROT))
    c[:, C_FREQ] = np.where(dim < ROT, freq[dim % (ROT // 2)], 0.0)
    c[:, C_SGN] = np.where(dim < ROT // 2, -1.0, np.where(dim < ROT, 1.0, 0.0))
    return c


def _blocks(w, width=P):
    k, n = w.shape
    return w.reshape(k // P, P, n // width, width).transpose(2, 1, 0, 3).reshape(n // width, P, k // P * width)


def kernel(x, positions, ffn1_norm, ffn1_w1, ffn1_w3, ffn1_w2, mix_norm, w_in, gla_w_a2, gla_b_a, gla_out_norm,
           att_out_norm, w_out, ffn2_norm, ffn2_w1, ffn2_w3, ffn2_w2, final_norm):
    import concourse.bacc as bacc
    from concourse.bass_utils import run_bass_kernel_spmd

    def col(v):
        return np.asarray(v).reshape(-1, P).T

    def ffn(w1, w3, w2):
        up = np.concatenate([_blocks(np.asarray(w1)[0]), _blocks(np.asarray(w3)[0])], axis=2)
        w2 = np.asarray(w2)[0]
        return up, [_blocks(w2[a * P:b * P]) for a, b in PARTS]

    def pairs(b):
        n, p, w = b.shape
        return b.reshape(n // 2, 2, p, w).transpose(0, 2, 1, 3).reshape(n // 2, p, 2 * w)

    def values(w):
        return w.reshape(2, 4, P, S).transpose(0, 2, 1, 3).reshape(2, P, 4 * S)

    w = np.asarray(w_in)[0]
    up1, (d1a, d1b) = ffn(ffn1_w1, ffn1_w3, ffn1_w2)
    up2, (d2a, d2b) = ffn(ffn2_w1, ffn2_w3, ffn2_w2)
    arrays = {
        "xT": np.asarray(x)[0].T.reshape(KC, P, S),
        "positions": np.asarray(positions).reshape(1, S),
        "gains": np.concatenate([col(v) for v in (ffn1_norm, mix_norm, ffn2_norm, final_norm, gla_out_norm,
                                                  att_out_norm, gla_b_a)], axis=1),
        "up1": up1, "down1a": d1a, "down1b": d1b,
        "w_proj": pairs(np.concatenate([_blocks(w[:, c:c + n]) for c, n in
                                        ((AQ, ATT_W), (AK, ATT_W), (GQ, GLA_KW), (GK, GLA_KW), (GR, GLA_W))])),
        "w_ga": _blocks(w[:, GA:GA + P])[0],
        "w_v": np.concatenate([values(w[:, AV:AV + ATT_W]), values(w[:, GV:GV + GLA_W])]),
        "w_a2": np.asarray(gla_w_a2)[0],
        "w_o": pairs(_blocks(np.asarray(w_out)[0])),
        "up2": up2, "down2a": d2a, "down2b": d2b,
        "const": _constants(),
    }
    arrays = {k: np.ascontiguousarray(v) for k, v in arrays.items()}
    nc = bacc.Bacc("TRN2", target_bir_lowering=False, num_devices=1)
    ap = {k: nc.dram_tensor("in_" + k, v.shape, mybir.dt.from_np(v.dtype), kind="ExternalInput").ap() for k, v in arrays.items()}
    outT = nc.dram_tensor("outT", (KC, P, S), F32, kind="ExternalOutput").ap()
    layer_program(nc, ap["xT"], ap["positions"], ap["gains"], ap["up1"], (ap["down1a"], ap["down1b"]), ap["w_proj"],
                  ap["w_ga"], ap["w_v"], ap["w_a2"], ap["w_o"], ap["up2"], (ap["down2a"], ap["down2b"]),
                  ap["const"], outT)
    r = run_bass_kernel_spmd(nc, [{"in_" + k: v for k, v in arrays.items()}], core_ids=[0])
    return r.results[0]["outT"].reshape(D, S).T.reshape(1, S, D)
```

```python
import math
from contextlib import ExitStack

import numpy as np

import concourse.bass as bass
from concourse import mybir

F32 = mybir.dt.float32
F32R = mybir.dt.float32r
I32 = mybir.dt.int32
U32 = mybir.dt.uint32
ALU = mybir.AluOpType
ACT = mybir.ActivationFunctionType

P = 128
D = 1024
S = 512
KC = D // P
ST = S // P
D_FF = 2816
FT = D_FF // P
PARTS = ((0, 12), (12, 22))
GLA_W, GLA_H, GLA_DV, GLA_DK, GLA_KW, GLA_RANK, CHUNK = 512, 4, 128, 64, 256, 16, 64
ATT_W, ATT_H, HD, ROT = 512, 8, 64, 16
NCH = S // CHUNK
EPS = 1e-6
THETA = 500000.0
PATTERNS = ((128, 1), (512, 4), (2048, 16))

GQ, GK, GV, GR, GA, AQ, AK, AV = 0, 256, 512, 1024, 1536, 1552, 2064, 2576
T_GQ, T_GK, T_GR, T_AQ, T_AK, T_GA = 0, 2, 4, 8, 9, 16

UP_W, A_W, V_W = 2 * D, 2 * D, 4 * S
FFN_UNITS = FT + 2 * KC
FFN_TILES = 2 * FT + 2 * KC
MIX_UNITS = 1 + 4 + 2 + 2 + 4 + 4
MIX_TILES = 1 + 16 + 8 + 8
BANK_CREDIT = 4

G_FFN1, G_MIX, G_FFN2, G_FINAL, G_GLA, G_ATT, G_BA = 0, 8, 16, 24, 32, 36, 40
N_GAINS = 42

C_ID, C_ONE, C_STRIP, C_TRI, C_SCAN, C_FREQ, C_SGN, C_EPS = 0, 128, 256, 768, 1280, 1792, 1793, 1794
N_CONST = 1795
AHEAD = 6
NORM = {0: 0, 2: 4}
MAGIC = 1.5 * 2.0 ** 23
TWO_PI = (6.28125, 0.00193500518798828125, 2 * math.pi - 6.28125 - 0.00193500518798828125)
SCORE_SCALE = HD ** -0.5
FAR = -1e30


def layer_program(nc, xT_in, positions, gains_in, up1, down1, w_proj, w_ga, w_v, w_a2, w_o, up2, down2,
                  const_in, outT):
    ctx = ExitStack()
    with ctx:
        def sb(name, shape, dt=F32, scope=ctx):
            return scope.enter_context(nc.sbuf_tensor(name, shape, dt))

        def sem(name):
            return ctx.enter_context(nc.semaphore(name))

        x = sb("x", [P, KC, S])
        h_hi = sb("h_hi", [P, KC, S], F32R)
        h_lo = sb("h_lo", [P, KC, S], F32R)
        raw = [sb(f"raw{j}", [P, UP_W]) for j in range(2)]
        w_hi = [sb(f"w_hi{j}", [P, UP_W], F32R) for j in range(2)]
        w_lo = [sb(f"w_lo{j}", [P, UP_W], F32R) for j in range(2)]
        const = sb("const", [P, N_CONST])
        gains = sb("gains", [P, N_GAINS, 1])
        credit = sb("credit", [P, 1])
        wa2 = sb("wa2", [GLA_RANK, GLA_KW])
        rstd = sb("rstd", [P, S])
        rstd_tok = sb("rstd_tok", [P, ST])
        nrm = sb("nrm", [P, 3, ST])
        sumsq = sb("sumsq", [P, S])
        square = sb("square", [P, S])
        rope_c = sb("rope_c", [P, S])
        rope_s = sb("rope_s", [P, S])
        ident = const[:, C_ID:C_ID + P]
        ones = const[:, C_ONE:C_ONE + P]

        def ffn_memory(n):
            scope = ExitStack()
            g_hi = sb(f"g_hi{n}", [P, PARTS[0][1], S], F32R, scope)
            g_lo = sb(f"g_lo{n}", [P, PARTS[0][1], S], F32R, scope)
            gate = sb(f"gate{n}", [P, S], F32, scope)
            prod = sb(f"prod{n}", [P, S], F32, scope)
            norm_diag = sb(f"norm_diag{n}", [P, ST, P], F32, scope) if n == 2 else None
            scope.close()
            return g_hi, g_lo, gate, prod, norm_diag

        ffn_mem = {1: ffn_memory(1)}
        mix = ExitStack()
        projT = sb("projT", [P, 17, S], F32, mix)
        v_att = sb("v_att", [P, ST, ATT_W], F32, mix)
        v_gla = sb("v_gla", [P, ST, GLA_W], F32, mix)
        gt = [[sb(f"gt{n}_{p}", [P, S], F32, mix) for p in range(2)] for n in range(3)]
        negm = sb("negm", [P, 4 * ATT_H], F32, mix)
        den = sb("den", [P, 4 * ATT_H], F32, mix)
        rden = sb("rden", [P, 4 * ATT_H], F32, mix)
        late = ExitStack()
        probs = [sb(f"probs{j}", [P, 10 * P], F32, late) for j in range(2)]
        probsT = [sb(f"probsT{j}", [P, ST, S], F32, late) for j in range(2)]
        NDIAG = 8
        diag = sb("diag", [P, NDIAG, P], F32, late)
        late.close()
        late = ExitStack()
        k_tok = [sb(f"k_tok{p}", [P, ST, P], F32, late) for p in range(2)]
        state = [sb(f"state{p}", [P, NCH, GLA_DV], F32, late) for p in range(2)]
        att_g = [sb(f"att_g{g}", [P, S], F32, late) for g in range(GLA_H)]
        late.close()
        mix.close()
        o_gla = [gt[1][0], gt[1][1], gt[2][0], gt[2][1]]
        sq_gla = [projT[:, T_GK, :], projT[:, T_GK + 1, :], gt[0][0][:], gt[0][1][:]]
        ffn_mem[2] = ffn_memory(2)
        early = ExitStack()
        sb("under_ffn1", [P, 2 * PARTS[0][1] * S + 2 * S], F32, early)
        pos_i = sb("pos_i", [P, S], I32, early)
        ang = sb("ang", [P, S], F32, early)
        turn = sb("turn", [P, S], F32, early)
        part = sb("part", [P, S], F32, early)
        early.close()

        ps = [ctx.enter_context(nc.psum_tensor(f"bank{b}", [P, S], F32)) for b in range(8)]

        x_in = [sem(f"x_in{j}") for j in range(4)]
        gains_in_sem = sem("gains_landed")
        const_landed = sem("const_landed")
        w_first = sem("w_first")
        pos_landed = sem("pos_landed")
        w_in = [sem(f"w_in{j}") for j in range(2)]
        first_round = sem("first_round")
        first_split = sem("first_split")
        first_sq = sem("first_sq")
        first_sum = sem("first_sum")
        w_round = sem("w_round")
        w_split = sem("w_split")
        tile_done = sem("tile_done")
        tile_out = sem("tile_out")
        v_half = sem("v_half")
        h_free = sem("h_free")
        h_round = sem("h_round")
        h_ready = sem("h_ready")
        sq_done = sem("sq_done")
        sq_added = sem("sq_added")
        sums_done = sem("sums_done")
        sums_out = sem("sums_out")
        root_done = sem("root_done")
        rstd_done = sem("rstd_done")
        silu_done = sem("silu_done")
        g_mul = sem("g_mul")
        g_round = sem("g_round")
        g_ready = sem("g_ready")
        pool_step = sem("pool_step")
        ang_sin = sem("ang_sin")
        rope_tab = sem("rope_tab")
        rope_scaled = sem("rope_scaled")
        rope_shuf = sem("rope_shuf")
        rope_cos = sem("rope_cos")
        rope_sin = sem("rope_sin")
        rope_done = sem("rope_done")
        z_done = sem("z_done")
        z_out = sem("z_out")
        act_step = sem("act_step")
        log_done = sem("log_done")
        gr_done = sem("gr_done")
        s_done = sem("s_done")
        s_masked = sem("s_masked")
        exp_done = sem("exp_done")
        rden_done = sem("rden_done")
        diag_done = sem("diag_done")
        pt_done = sem("pt_done")
        pt_out = sem("pt_out")
        o_done = sem("o_done")
        o_out = sem("o_out")
        dve_step = sem("dve_step")
        b_done = sem("b_done")
        eb_done = sem("eb_done")
        tail_done = sem("tail_done")
        et_done = sem("et_done")
        gla_ready = sem("gla_ready")
        ktail_done = sem("ktail_done")
        ktail_out = sem("ktail_out")
        att_squares = sem("att_squares")
        og_copied = sem("og_copied")
        og_squared = sem("og_squared")
        gla_sums_done = sem("gla_sums_done")
        gla_ln = sem("gla_ln")
        gla_rstd = sem("gla_rstd")
        gla_half = sem("gla_half")
        norm_diag_done = sem("norm_diag_done")
        rstd_wide = sem("rstd_wide")
        ag_done = sem("ag_done")
        ag_out = sem("ag_out")
        u_done = sem("u_done")
        state_done = sem("state_done")
        og_done = sem("og_done")
        att_scaled = sem("att_scaled")
        gla_scaled = sem("gla_scaled")
        fin_done = sem("fin_done")
        stored = sem("stored")

        block = ctx.enter_context(nc.Block())

        first_squares = [sumsq, square, rstd, ffn_mem[1][2]]

        U_MIX, U_FFN2 = FFN_UNITS, FFN_UNITS + MIX_UNITS
        T_MIX, T_FFN2 = FFN_TILES, FFN_TILES + MIX_TILES
        N_UNITS = 2 * FFN_UNITS + MIX_UNITS

        def ffn_phases(u0, t0):
            out = []
            for a, b in PARTS:
                out.append(("up", u0, t0, b - a, a))
                u0, t0 = u0 + b - a, t0 + 2 * (b - a)
                out.append(("down", u0, t0, KC, a))
                u0, t0 = u0 + KC, t0 + KC
            return out

        def hidden(phase):
            return next(b - a for a, b in PARTS if a == phase[4])

        def unit_size(u):
            for base in (0, U_FFN2):
                if base <= u < base + FFN_UNITS:
                    for kind, u0, _, n, a in ffn_phases(base, 0):
                        if u0 <= u < u0 + n:
                            return UP_W if kind == "up" else P * next(b - c for c, b in PARTS if c == a)
            return D if u == U_MIX else UP_W

        @block.sync
        def _(sp):
            def load(u, i, src):
                if not (isinstance(i, int) and u + 2 * i < 2):
                    sp.wait_ge(w_split, u - 1 + 2 * i)
                sp.dma_start(raw[u % 2][:, 0:src.shape[-1]], src).then_inc(w_in[u % 2], 16)

            def phase(u0, n, source):
                peeled = u0 == 0
                if peeled:
                    sp.dma_start(raw[0][:, 0:D], source(0)[:, 0:D]).then_inc(w_first, 16)
                    for j in range(4):
                        sp.dma_start(x[:, 2 * j:2 * j + 2, :],
                                     xT_in[2 * j:2 * j + 2].rearrange("c p s -> p c s")).then_inc(x_in[j], 16)
                    sp.dma_start(raw[0][:, D:UP_W], source(0)[:, D:UP_W]).then_inc(w_in[0], 16)
                    load(1, 0, source(1))
                    sp.dma_start(const[:], const_in).then_inc(const_landed, 16)
                    sp.dma_start(wa2[:], w_a2).then_inc(const_landed, 16)
                    sp.dma_start(pos_i[:], positions.partition_broadcast(P)).then_inc(pos_landed, 16)
                with sp.Fori(int(peeled), n // 2) as i:
                    for j in range(2):
                        load(u0 + j, i, source(2 * i + j))

            def ffn(base, up, down):
                for kind, u0, _, n, a in ffn_phases(base, 0):
                    if kind == "up":
                        phase(u0, n, lambda f: up[f + a])
                    else:
                        phase(u0, n, lambda m: down[0 if a == 0 else 1][m])

            ffn(0, up1, down1)
            load(U_MIX, 0, w_ga)
            phase(U_MIX + 1, 4, lambda n: w_proj[n])
            phase(U_MIX + 5, 4, lambda n: w_v[n])
            phase(U_MIX + 9, 4, lambda n: w_proj[n + 4])
            phase(U_MIX + 13, 4, lambda n: w_o[n])
            ffn(U_FFN2, up2, down2)
            for m in range(0, KC, 2):
                sp.wait_ge(fin_done, m + 1)
                sp.dma_start(outT[m], x[:, m, :]).then_inc(stored, 16)
            sp.wait_ge(stored, 16 * KC)

        @block.gpsimd
        def _(pool):
            count = [0]

            def step(ins):
                count[0] += 1
                ins.then_inc(pool_step, 1)
                pool.wait_ge(pool_step, count[0])

            for m in range(KC // 2, KC):
                pool.wait_ge(x_in[m // 2], 16)
                if m == KC // 2:
                    step(nc.gpsimd.tensor_tensor(rope_s[:], x[:, m, :], x[:, m, :], ALU.mult))
                else:
                    step(nc.gpsimd.tensor_tensor(part[:], x[:, m, :], x[:, m, :], ALU.mult))
                    step(nc.gpsimd.tensor_tensor(rope_s[:], rope_s[:], part[:], ALU.add))
            pool.wait_ge(sums_done, 1)
            pool.wait_ge(pos_landed, 16)
            pool.wait_ge(const_landed, 32)
            step(nc.gpsimd.tensor_copy(ang[:], pos_i[:]))
            step(nc.gpsimd.tensor_scalar(ang[:], ang[:], const[:, C_FREQ:C_FREQ + 1], None, ALU.mult))
            for table, quarter in ((rope_s, 0.0), (rope_c, 0.25)):
                step(nc.gpsimd.tensor_scalar(turn[:], ang[:], 1 / (2 * math.pi), quarter, ALU.mult, ALU.add))
                step(nc.gpsimd.tensor_scalar(turn[:], turn[:], MAGIC, None, ALU.add))
                step(nc.gpsimd.tensor_scalar(turn[:], turn[:], -MAGIC, None, ALU.add))
                left = ang
                for c in TWO_PI:
                    step(nc.gpsimd.tensor_scalar(part[:], turn[:], c, None, ALU.mult))
                    step(nc.gpsimd.tensor_tensor(table[:], left[:], part[:], ALU.subtract))
                    left = table
                if quarter:
                    step(nc.gpsimd.tensor_scalar(table[:], table[:], math.pi / 2, None, ALU.add))
                last = nc.gpsimd.tensor_scalar(table[:], table[:], 3.1415925, -3.1415925, ALU.min, ALU.max)
                last.then_inc(ang_sin, 1)
            for n in range(2 * ST):
                pool.wait_ge(rope_scaled, 2)
                pool.wait_ge(rope_shuf, n + 1)
                t = T_AQ + n
                nc.gpsimd.tensor_tensor(projT[:, t, :], projT[:, t, :], rope_c[:], ALU.mult).then_inc(rope_cos, 1)
            pool.wait_ge(rope_done, 2 * ST)
            for n in range(3):
                pool.wait_ge(o_out, 2 * n + 2)
                o = projT[:, T_AQ + 2 * n, :]
                if n == 0:
                    nc.gpsimd.tensor_tensor(rope_s[:], o, o, ALU.mult).then_inc(att_squares, 1)
                else:
                    pool.wait_ge(att_squares, n)
                    step(nc.gpsimd.tensor_tensor(rope_c[:], o, o, ALU.mult))
                    nc.gpsimd.tensor_tensor(rope_s[:], rope_s[:], rope_c[:], ALU.add).then_inc(att_squares, 1)

        @block.scalar
        def _(act):
            def split(u, i, size):
                act.wait_ge(w_in[u % 2], 16 * (u // 2 + 1) + 16 * i)
                nc.scalar.activation(w_hi[u % 2][:, 0:size], raw[u % 2][:, 0:size], ACT.Copy).then_inc(w_round, 1)

            def split_next(u, i, tiles):
                if isinstance(i, int):
                    u, i = u + 2 * i, 0
                if u + 2 < N_UNITS:
                    act.wait_ge(tile_done, tiles)
                    split(u + 2, i, unit_size(u + 2))

            def round_h(layer, m, col):
                nc.scalar.activation(h_hi[:, m, :], x[:, m, :], ACT.Copy,
                                     scale=gains[:, col + m, :]).then_inc(h_round, 1)

            def square_x(layer, m):
                act.wait_ge(sq_added, 9 * (layer - 1) + 1 + m)
                act.nop(nofuse=True)
                nc.scalar.activation(square[:], x[:, m, :], ACT.Square).then_inc(sq_done, 1)

            def root(n):
                act.wait_ge(sums_out, n + 1)
                nc.scalar.activation(rstd[:], rstd[:], ACT.Sqrt).then_inc(root_done, 1)

            def ffn(layer, base, tbase, g_hi, gate, prod, next_gain):
                gb = FT * (layer // 2)
                for kind, u0, t0, n, a in ffn_phases(base, tbase):
                    def up(i, j):
                        f = 2 * i + j
                        t = t0 + 2 * f
                        act.wait_ge(tile_out, BANK_CREDIT + t + 1)
                        nc.scalar.activation(gate[:], gate[:], ACT.Silu).then_inc(silu_done, 1)
                        split_next(u0 + j, i, t + 2)
                        act.wait_ge(g_mul, gb + a + f + 1)
                        nc.scalar.activation(g_hi[:, f, :], prod[:], ACT.Copy).then_inc(g_round, 1)

                    def down(i, j):
                        m = 2 * i + j
                        if a:
                            act.wait_ge(tile_out, BANK_CREDIT + t0 + m + 1)
                            if layer == 0:
                                round_h(1, m, next_gain)
                            square_x(layer + 1, m)
                        split_next(u0 + j, i, t0 + m + 1)

                    step = up if kind == "up" else down
                    if kind == "up" and a == 0:
                        root(NORM[layer])
                    if kind == "down" and a and layer == 2:
                        nc.scalar.activation(credit[:], credit[:], ACT.Sqrt)
                    with act.Fori(0, n // 2 - 1) as i:
                        for j in range(2):
                            step(i, j)
                    for j in range(2):
                        step(n // 2 - 1, j)

            act.dma_start(gains[:].rearrange("p n a -> p (n a)"), gains_in).then_inc(gains_in_sem, 16)
            act.wait_ge(w_first, 16)
            nc.scalar.activation(w_hi[0][:, 0:D], raw[0][:, 0:D], ACT.Copy).then_inc(first_round, 1)
            act.wait_ge(gains_in_sem, 16)
            for m in range(KC):
                act.wait_ge(x_in[m // 2], 16)
                round_h(0, m, G_FFN1)
            act.wait_ge(w_in[0], 16)
            nc.scalar.activation(w_hi[0][:, D:UP_W], raw[0][:, D:UP_W], ACT.Copy).then_inc(w_round, 1)
            for m, out in enumerate(first_squares):
                nc.scalar.activation(out[:], x[:, m, :], ACT.Square).then_inc(first_sq, 1)
            split(1, 0, unit_size(1))
            ffn(0, 0, 0, ffn_mem[1][0], ffn_mem[1][2], ffn_mem[1][3], G_MIX)

            act.wait_ge(ang_sin, 2)
            nc.scalar.activation(rope_s[:], rope_s[:], ACT.Sin).then_inc(rope_tab, 1)
            nc.scalar.activation(rope_c[:], rope_c[:], ACT.Sin).then_inc(rope_tab, 1)
            root(1)
            act.wait_ge(sums_out, 3)
            nc.scalar.activation(rstd_tok[:], rstd_tok[:], ACT.Sqrt).then_inc(root_done, 1)
            U, T = U_MIX, T_MIX
            split_next(U, 0, T + 1)
            split_next(U + 1, 0, T + 3)
            for p in range(2):
                act.wait_ge(z_done, p + 1)
                nc.scalar.activation(gt[0][p][:], ps[5 - p][:], ACT.Identity,
                                     bias=gains[:, G_BA + p, :]).then_inc(z_out, 1)
            for p in range(2):
                act.wait_ge(z_out, p + 1)
                nc.scalar.activation(gt[1][p][:], gt[0][p][:], ACT.Abs).then_inc(act_step, 1)
            for p in range(2):
                act.wait_ge(act_step, p + 1)
                nc.scalar.activation(gt[1][p][:], gt[1][p][:], ACT.Exp, scale=-1.0).then_inc(act_step, 1)
            for p in range(2):
                act.wait_ge(act_step, p + 3)
                nc.scalar.activation(gt[1][p][:], gt[1][p][:], ACT.Ln, bias=ones[:, 0:1]).then_inc(log_done, 1)
            split_next(U + 2, 0, T + 5)
            for p in range(2):
                act.wait_ge(b_done, p + 1)
                nc.scalar.activation(gt[0][p][:], gt[1][p][:], ACT.Exp, scale=1 / 16).then_inc(eb_done, 1)
                nc.scalar.activation(gt[2][p][:], gt[1][p][:], ACT.Exp, scale=-1 / 16).then_inc(eb_done, 1)
                act.wait_ge(tail_done, p + 1)
                act.wait_ge(eb_done, 2 * p + 2)
                nc.scalar.activation(gt[1][p][:], square[:], ACT.Exp, scale=1 / 16).then_inc(et_done, 1)
            split_next(U + 3, 0, T + 7)
            split_next(U + 4, 0, T + 9)
            for n in range(4):
                act.wait_ge(tile_out, BANK_CREDIT + T + 9)
                nc.scalar.activation(projT[:, T_GR + n, :], projT[:, T_GR + n, :], ACT.Silu).then_inc(gr_done, 1)
            for p in range(2):
                act.wait_ge(ktail_done, p + 1)
                nc.scalar.activation(k_tok[p][:].rearrange("p t c -> p (t c)"), ps[p][:], ACT.Copy).then_inc(ktail_out, 1)
            act.wait_ge(v_half, 1)
            split(U + 7, 0, unit_size(U + 7))
            split_next(U + 6, 0, T + 13)
            act.wait_ge(v_half, 2)
            split(U + 9, 0, unit_size(U + 9))
            split_next(U + 8, 0, T + 17)
            def move_tiles(n):
                for w in range(2):
                    t = T + 17 + 2 * n + w
                    act.wait_ge(tile_done, t + 1)
                    act.wait_ge(tile_out, BANK_CREDIT + t)
                    nc.scalar.activation(projT[:, T_AQ + 2 * n + w, :], ps[2 * (n % 2) + w][:],
                                         ACT.Copy).then_inc(tile_out, 1)

            for g in range(GLA_H):
                act.wait_ge(og_done, g + 1)
                nc.scalar.activation(o_gla[g][:], ps[4 + g][:], ACT.Copy).then_inc(og_copied, 1)
                nc.scalar.activation(sq_gla[g], ps[4 + g][:], ACT.Square).then_inc(og_squared, 1)
            move_tiles(0)
            split_next(U + 9, 0, T + 19)
            for g in range(GLA_H):
                act.wait_ge(gla_sums_done, g + 1)
                nc.scalar.activation(sq_gla[g], ps[4 + g][:], ACT.Ln, bias=const[:, C_EPS:C_EPS + 1],
                                     scale=1.0 / GLA_DV).then_inc(gla_ln, 1)
            for g in range(GLA_H):
                act.wait_ge(gla_ln, g + 1)
                nc.scalar.activation(sq_gla[g], sq_gla[g], ACT.Exp, scale=-0.5).then_inc(gla_rstd, 1)
            move_tiles(1)
            split_next(U + 10, 0, T + 21)

            def exp_scores(q):
                h, i = q // 4, q % 4
                off = P * i * (i + 1) // 2
                strip = probs[h % 2][:, off:off + P * (i + 1)]
                act.wait_ge(s_masked, q + 1)
                nc.scalar.activation(strip, strip, ACT.Exp, bias=negm[:, q:q + 1], scale=-1.0,
                                     accum_out=den[:, q:q + 1]).then_inc(exp_done, 1)

            def move_probsT(h, i):
                act.wait_ge(pt_done, 4 * h + i + 1)
                if h >= 2:
                    act.wait_ge(o_done, h - 1)
                nc.scalar.activation(probsT[h % 2][:, 0:i + 1, i * P:(i + 1) * P],
                                     ps[i][:, 0:(i + 1) * P].rearrange("p (j q) -> p j q", q=P),
                                     ACT.Copy).then_inc(pt_out, 1)

            def high_concat(g):
                act.wait_ge(tile_done, T + 25)
                act.wait_ge(gla_scaled, g + 1)
                nc.scalar.activation(h_hi[:, g, :], o_gla[g][:], ACT.Copy).then_inc(h_round, 1)

            exp_scores(0)
            exp_scores(1)
            move_tiles(2)
            split_next(U + 11, 0, T + 23)
            exp_scores(2)
            exp_scores(3)
            exp_scores(4)
            exp_scores(5)
            move_tiles(3)
            for h in range(ATT_H):
                for i in range(4):
                    if 4 * h + i + AHEAD < 4 * ATT_H:
                        exp_scores(4 * h + i + AHEAD)
                    move_probsT(h, i)
                if h == ATT_H - 2:
                    split_next(U + 12, 0, T + 25)
                if 2 <= h <= 5:
                    high_concat(h - 2)
            act.wait_ge(sums_out, 4)
            nc.scalar.activation(nrm[:, 1, :], nrm[:, 0, :], ACT.Sqrt).then_inc(root_done, 1)
            for k in range(4):
                act.wait_ge(att_scaled, k + 1)
                nc.scalar.activation(h_hi[:, 4 + k, :], projT[:, T_AQ + 2 * k, :], ACT.Copy).then_inc(h_round, 1)
            UO, TO = U + 13, T + 25
            for n in range(3):
                split_next(UO + n, 0, TO + 2 * n + 2)
                for m in (2 * n, 2 * n + 1):
                    act.wait_ge(tile_out, BANK_CREDIT + TO + m + 1)
                    square_x(2, m)
            act.wait_ge(tile_out, BANK_CREDIT + TO + 7)
            square_x(2, 6)
            for m in range(KC):
                if m < KC - 1:
                    act.wait_ge(h_free, m + 1)
                else:
                    act.wait_ge(tile_out, BANK_CREDIT + TO + 8)
                round_h(2, m, G_FFN2)
            square_x(2, 7)
            split_next(UO + 3, 0, TO + 8)
            ffn(2, U_FFN2, T_FFN2, ffn_mem[2][0], ffn_mem[2][2], ffn_mem[2][3], None)
            act.wait_ge(sums_out, 6)
            nc.scalar.activation(nrm[:, 1, :], nrm[:, 0, :], ACT.Sqrt).then_inc(root_done, 1)
            for m in range(1, KC, 2):
                act.wait_ge(fin_done, m + 1)
                act.dma_start(outT[m], x[:, m, :]).then_inc(stored, 16)

        @block.vector
        def _(dve):
            def split(u, i, size):
                dve.wait_ge(w_round, u + 1 + 2 * i)
                nc.vector.tensor_tensor(w_lo[u % 2][:, 0:size], raw[u % 2][:, 0:size],
                                        w_hi[u % 2][:, 0:size].bitcast(F32), ALU.subtract).then_inc(w_split, 1)

            def split_next(u, i):
                if isinstance(i, int):
                    u, i = u + 2 * i, 0
                if u + 2 < N_UNITS:
                    split(u + 2, i, unit_size(u + 2))

            def low_h(count, m, col):
                dve.wait_ge(h_round, count + 1)
                nc.vector.scalar_tensor_tensor(h_lo[:, m, :], x[:, m, :], gains[:, col + m, :],
                                               h_hi[:, m, :].bitcast(F32), ALU.mult, ALU.subtract).then_inc(h_ready, 1)

            def clear_sums():
                nc.vector.memset(sumsq[:], 0.0).then_inc(sq_added, 1)

            def add_square(layer, m):
                dve.wait_ge(sq_done, 8 * (layer - 1) + m + 1)
                dve.wait_ge(sq_added, 9 * (layer - 1) + m + 1)
                nc.vector.tensor_tensor(sumsq[:], sumsq[:], square[:], ALU.add).then_inc(sq_added, 1)

            def mean_square(n, bank, width, out):
                dve.wait_ge(sums_done, n + 1)
                nc.vector.tensor_scalar(out, bank, 1.0 / width, EPS, ALU.mult, ALU.add).then_inc(sums_out, 1)

            def reciprocal_root(n, out):
                dve.wait_ge(root_done, n + 1)
                nc.vector.reciprocal(out, out).then_inc(rstd_done, 1)
                dve.wait_ge(rstd_done, n + 1)

            def ffn(layer, base, tbase, g_hi, g_lo, gate, prod, norm_diag, next_gain):
                gb = FT * (layer // 2)
                for kind, u0, t0, n, a in ffn_phases(base, tbase):
                    def up(i, j):
                        f = 2 * i + j
                        t = t0 + 2 * f
                        dve.wait_ge(tile_done, t + 1)
                        nc.vector.tensor_tensor(gate[:], ps[2 * j][:], rstd[:], ALU.mult).then_inc(tile_out, 1)
                        dve.wait_ge(tile_done, t + 2)
                        nc.vector.tensor_tensor(prod[:], ps[2 * j + 1][:], rstd[:], ALU.mult).then_inc(tile_out, 1)
                        dve.wait_ge(silu_done, gb + a + f + 1)
                        dve.wait_ge(tile_out, BANK_CREDIT + t + 2)
                        nc.vector.tensor_tensor(prod[:], prod[:], gate[:], ALU.mult).then_inc(g_mul, 1)
                        split_next(u0 + j, i)
                        dve.wait_ge(g_round, gb + a + f + 1)
                        nc.vector.tensor_tensor(g_lo[:, f, :], prod[:], g_hi[:, f, :].bitcast(F32),
                                                ALU.subtract).then_inc(g_ready, 1)
                        dve.wait_ge(g_ready, gb + a + f + 1)

                    def down(i, j):
                        m = 2 * i + j
                        dve.wait_ge(tile_done, t0 + m + 1)
                        nc.vector.scalar_tensor_tensor(x[:, m, :], ps[4 + j][:], 0.5, x[:, m, :],
                                                       ALU.mult, ALU.add).then_inc(tile_out, 1)
                        if a:
                            if layer == 0:
                                low_h(8 + m, m, next_gain)
                            if not (layer == 2 and isinstance(i, int) and m == KC - 1):
                                add_square(layer + 1, m)
                        split_next(u0 + j, i)

                    step = up if kind == "up" else down
                    if kind == "up" and a == 0:
                        mean_square(NORM[layer], ps[6][:], D, rstd[:])
                        reciprocal_root(NORM[layer], rstd[:])
                        clear_sums()
                    with dve.Fori(0, n // 2 - 1) as i:
                        for j in range(2):
                            step(i, j)
                    for j in range(2):
                        step(n // 2 - 1, j)

            nc.vector.memset(credit[:], 0.0).then_inc(tile_out, BANK_CREDIT)
            dve.wait_ge(first_round, 1)
            nc.vector.tensor_tensor(w_lo[0][:, 0:D], raw[0][:, 0:D], w_hi[0][:, 0:D].bitcast(F32),
                                    ALU.subtract).then_inc(first_split, 1)
            for m in range(KC):
                low_h(m, m, G_FFN1)
            dve.wait_ge(w_round, 1)
            nc.vector.tensor_tensor(w_lo[0][:, D:UP_W], raw[0][:, D:UP_W], w_hi[0][:, D:UP_W].bitcast(F32),
                                    ALU.subtract).then_inc(w_split, 1)
            for m in range(1, KC // 2):
                dve.wait_ge(first_sq, m + 1)
                if m > 1:
                    dve.wait_ge(first_sum, m - 1)
                nc.vector.tensor_tensor(sumsq[:], sumsq[:], first_squares[m][:], ALU.add).then_inc(first_sum, 1)
            split(1, 0, unit_size(1))
            ffn(0, 0, 0, *ffn_mem[1], G_MIX)

            steps = [0]

            def chain(ins):
                steps[0] += 1
                ins.then_inc(dve_step, 1)
                dve.wait_ge(dve_step, steps[0])

            mean_square(1, ps[6][:], D, rstd[:])
            mean_square(2, ps[7][:, 0:ST], D, rstd_tok[:])
            reciprocal_root(1, rstd[:])
            reciprocal_root(2, rstd_tok[:])
            U, T = U_MIX, T_MIX
            dve.wait_ge(tile_done, T + 1)
            nc.vector.tensor_tensor(projT[:, T_GA, :], ps[4][:], rstd[:], ALU.mult).then_inc(tile_out, 1)
            split_next(U, 0)

            def project(unit, tile, t):
                for w in range(2):
                    dve.wait_ge(tile_done, t + w + 1)
                    nc.vector.tensor_tensor(projT[:, tile + w, :], ps[2 * ((unit + 1) % 2) + w][:], rstd[:],
                                            ALU.mult).then_inc(tile_out, 1)

            def values_out(values, banks, t0):
                for t in range(ST):
                    dve.wait_ge(tile_done, t0 + t + 1)
                    nc.vector.tensor_scalar(values[:, t, :], ps[banks[t]][:], rstd_tok[:, t:t + 1], None,
                                            ALU.mult).then_inc(tile_out, 1)

            def rotate(n):
                t = T_AQ + n
                dve.wait_ge(tile_out, BANK_CREDIT + T + 17 + n + 1)
                if n == 0:
                    dve.wait_ge(et_done, 2)
                if n > 1:
                    dve.wait_ge(rope_done, n - 1)
                half = ROT // 2
                shuffled = (square, sumsq)[n % 2]
                nc.vector.stream_shuffle(shuffled[:], projT[:, t, :],
                                         [(c + half) % ROT if c < ROT else c for c in range(32)]).then_inc(rope_shuf, 1)
                dve.wait_ge(rope_shuf, n + 1)
                nc.vector.tensor_tensor(shuffled[:], shuffled[:], rope_s[:], ALU.mult).then_inc(rope_sin, 1)

            def rotated(n):
                t = T_AQ + n
                dve.wait_ge(rope_sin, n + 1)
                dve.wait_ge(rope_cos, n + 1)
                nc.vector.tensor_tensor(projT[:, t, :], projT[:, t, :], (square, sumsq)[n % 2][:],
                                        ALU.add).then_inc(rope_done, 1)

            def rotate_pair(n):
                rotate(2 * n)
                rotate(2 * n + 1)
                rotated(2 * n)
                rotated(2 * n + 1)

            def mask_scores(q):
                h, i = q // 4, q % 4
                off, width = P * i * (i + 1) // 2, P * (i + 1)
                dve.wait_ge(s_done, q + 1)
                if h >= 2:
                    dve.wait_ge(pt_done, 4 * (h - 2) + i + 1)
                nc.vector.tensor_tensor_reduce(out=probs[h % 2][:, off:off + width], in0=ps[4 + i % 2][:, 0:width],
                                               in1=const[:, C_STRIP + S - width:C_STRIP + S],
                                               scale=-SCORE_SCALE, scalar=3e38, op0=ALU.add, op1=ALU.min,
                                               accum_out=negm[:, q:q + 1]).then_inc(s_masked, 1)

            def scaled_identity(q):
                dve.wait_ge(exp_done, q + 1)
                nc.vector.reciprocal(rden[:, q:q + 1], den[:, q:q + 1]).then_inc(rden_done, 1)
                dve.wait_ge(rden_done, q + 1)
                if q >= NDIAG:
                    dve.wait_ge(pt_done, q - NDIAG + 1)
                nc.vector.tensor_scalar(diag[:, q % NDIAG, :], ident, rden[:, q:q + 1], None,
                                        ALU.mult).then_inc(diag_done, 1)

            def move_out(h):
                r = HD * (h % 2)
                dve.wait_ge(o_done, h + 1)
                nc.vector.tensor_copy(projT[r:r + HD, T_AQ + 2 * (h // 2), :], ps[6 + h % 2][r:r + HD, :]).then_inc(o_out, 1)

            def gla_cumsum(p):
                dve.wait_ge(log_done, p + 1)
                chain(nc.vector.scalar_tensor_tensor(gt[0][p][:], gt[0][p][:], 0.0, gt[1][p][:], ALU.min, ALU.subtract))
                nc.vector.tensor_tensor_scan(gt[1][p][:], const[:, C_SCAN:C_SCAN + S], gt[0][p][:], 0.0,
                                             ALU.mult, ALU.add).then_inc(b_done, 1)

            def gla_decay(p):
                dve.wait_ge(b_done, p + 1)
                if p:
                    dve.wait_ge(et_done, p)
                b = gt[1][p][:].rearrange("p (c t) -> p c t", t=CHUNK)
                nc.vector.tensor_tensor(square[:].rearrange("p (c t) -> p c t", t=CHUNK),
                                        b[:, :, CHUNK - 1:CHUNK].broadcast_to([P, NCH, CHUNK]), b,
                                        ALU.subtract).then_inc(tail_done, 1)

            def gla_scale(p):
                dve.wait_ge(et_done, p + 1)
                nc.vector.tensor_tensor(gt[1][p][:], projT[:, T_GK + p, :], gt[1][p][:], ALU.mult).then_inc(gla_ready, 1)
                nc.vector.tensor_tensor(projT[:, T_GK + p, :], projT[:, T_GK + p, :], gt[2][p][:],
                                        ALU.mult).then_inc(gla_ready, 1)
                nc.vector.scalar_tensor_tensor(projT[:, T_GQ + p, :], projT[:, T_GQ + p, :], GLA_DK ** -0.5,
                                               gt[0][p][:], ALU.mult, ALU.mult).then_inc(gla_ready, 1)

            def gla_scores_out(g, bank):
                dve.wait_ge(ag_done, g + 1)
                nc.vector.copy_predicated(att_g[g][:], const[:, C_TRI:C_TRI + S].bitcast(U32),
                                          ps[bank][:]).then_inc(ag_out, 1)

            def gla_states():
                dve.wait_ge(u_done, 2 * (NCH - 1))
                for c in range(NCH - 1):
                    for p in range(2):
                        u = ps[4 + 2 * p + c % 2][:, (c // 2) * P:(c // 2 + 1) * P]
                        if c == 0:
                            ins = nc.vector.tensor_copy(state[p][:, 1, :], u)
                        else:
                            dve.wait_ge(state_done, 2 * c + p - 1)
                            ins = nc.vector.scalar_tensor_tensor(
                                state[p][:, c + 1, :], state[p][:, c, :],
                                gt[0][p][:, c * CHUNK + CHUNK - 1:c * CHUNK + CHUNK], u, ALU.mult, ALU.add)
                        ins.then_inc(state_done, 1)

            def gla_head_norm(g):
                o = o_gla[g][:]
                dve.wait_ge(gla_rstd, g + 1)
                dve.wait_ge(og_copied, g + 1)
                nc.vector.tensor_tensor(o, o, sq_gla[g], ALU.mult).then_inc(gla_half, 1)

            def gla_gated_output(g):
                o = o_gla[g][:]
                dve.wait_ge(gla_half, g + 1)
                dve.wait_ge(gr_done, 4)
                nc.vector.scalar_tensor_tensor(o, o, gains[:, G_GLA + g, :], projT[:, T_GR + g, :],
                                               ALU.mult, ALU.mult).then_inc(gla_scaled, 1)

            def low_concat(pos, k, tile):
                dve.wait_ge(h_round, 16 + pos + 1)
                nc.vector.tensor_tensor(h_lo[:, k, :], tile, h_hi[:, k, :].bitcast(F32), ALU.subtract).then_inc(h_ready, 1)

            def narrow_norm(n, k, bank, width, diags):
                v, y, z = nrm[:, 0, :], nrm[:, 1, :], nrm[:, 2, :]
                mean_square(n, ps[bank][:, 0:ST], width, v)
                reciprocal_root(n, y)
                chain(nc.vector.tensor_tensor(z, y, y, ALU.mult))
                chain(nc.vector.scalar_tensor_tensor(z, z, -0.5, v, ALU.mult, ALU.mult))
                chain(nc.vector.scalar_tensor_tensor(y, z, 1.5, y, ALU.add, ALU.mult))
                for t in range(ST):
                    last = nc.vector.tensor_scalar(diags[:, t, :], ident, y[:, t:t + 1], None, ALU.mult)
                    last.then_inc(norm_diag_done, 1)

            for g in range(GLA_H):
                nc.vector.memset(att_g[g][:], 0.0).then_inc(dve_step, 1)
            steps[0] += GLA_H
            project(1, T_GQ, T + 1)
            split_next(U + 1, 0)
            project(2, T_GK, T + 3)
            split_next(U + 2, 0)
            gla_cumsum(0)
            gla_cumsum(1)
            gla_decay(0)
            gla_scale(0)
            gla_decay(1)
            project(3, T_GR, T + 5)
            split_next(U + 3, 0)
            gla_scale(1)
            dve.wait_ge(rope_tab, 2)
            nc.vector.scalar_tensor_tensor(rope_s[:], rope_s[:], const[:, C_SGN:C_SGN + 1], rstd[:],
                                           ALU.mult, ALU.mult).then_inc(rope_scaled, 1)
            nc.vector.tensor_tensor(rope_c[:], rope_c[:], rstd[:], ALU.mult).then_inc(rope_scaled, 1)
            dve.wait_ge(rope_scaled, 2)
            project(4, T_GR + 2, T + 7)
            split_next(U + 4, 0)
            dve.wait_ge(dve_step, steps[0])
            gla_scores_out(0, 2)
            gla_scores_out(1, 3)
            split_next(U + 5, 0)
            values_out(v_gla, (4, 5, 6, 7), T + 9)
            gla_scores_out(2, 0)
            gla_scores_out(3, 1)
            split_next(U + 6, 0)
            split_next(U + 7, 0)
            gla_states()
            values_out(v_att, (2, 3, 0, 1), T + 13)
            split_next(U + 8, 0)
            split_next(U + 9, 0)
            rotate_pair(0)
            split_next(U + 10, 0)
            mask_scores(0)
            mask_scores(1)
            rotate_pair(1)
            split_next(U + 11, 0)
            mask_scores(2)
            scaled_identity(0)
            mask_scores(3)
            scaled_identity(1)
            scaled_identity(2)
            rotate_pair(2)
            mask_scores(4)
            scaled_identity(3)
            mask_scores(5)
            for h in range(ATT_H):
                for i in range(4):
                    q = 4 * h + i + AHEAD
                    if q < 4 * ATT_H:
                        mask_scores(q)
                    if q - 2 < 4 * ATT_H:
                        scaled_identity(q - 2)
                    if h == 1 and i < 2:
                        rotate(6 + i)
                    elif h == 1:
                        rotated(4 + i)
                    if i == 2 and h:
                        move_out(h - 1)
                    if i == 0 and 2 <= h <= 5:
                        gla_head_norm(h - 2)
                    if i == 1 and 2 <= h <= 5:
                        gla_gated_output(h - 2)
                    if i == 3 and 3 <= h <= 6:
                        low_concat(h - 3, h - 3, o_gla[h - 3][:])
                if h == ATT_H - 2:
                    split_next(U + 12, 0)
            move_out(ATT_H - 1)
            o = projT[:, T_AQ + 6, :]
            dve.wait_ge(o_out, ATT_H)
            chain(nc.vector.tensor_tensor(square[:], o, o, ALU.mult))
            dve.wait_ge(att_squares, 3)
            nc.vector.tensor_tensor(rope_s[:], rope_s[:], square[:], ALU.add).then_inc(att_squares, 1)
            dve.wait_ge(pt_done, 4 * ATT_H)
            narrow_norm(3, 0, 4, ATT_W, diag)
            for k in range(4):
                dve.wait_ge(rstd_wide, 1)
                o = projT[:, T_AQ + 2 * k, :]
                nc.vector.scalar_tensor_tensor(o, o, gains[:, G_ATT + k, :], ps[5][:],
                                               ALU.mult, ALU.mult).then_inc(att_scaled, 1)
                if k:
                    low_concat(3 + k, 3 + k, projT[:, T_AQ + 2 * k - 2, :])
            low_concat(7, 7, projT[:, T_AQ + 6, :])
            clear_sums()
            UO, TO = U + 13, T + 25
            for m in range(KC):
                if m == KC - 1:
                    for k in range(KC - 1):
                        low_h(24 + k, k, G_FFN2)
                dve.wait_ge(tile_done, TO + m + 1)
                nc.vector.tensor_tensor(x[:, m, :], x[:, m, :], ps[m % 4][:], ALU.add).then_inc(tile_out, 1)
                if m == KC - 1:
                    low_h(24 + m, m, G_FFN2)
                if m % 2 and m < KC - 1:
                    split_next(UO + m // 2, 0)
                add_square(2, m)
            split_next(UO + 3, 0)
            ffn(2, U_FFN2, T_FFN2, *ffn_mem[2], None)
            narrow_norm(5, 1, 7, D, ffn_mem[2][4])
            dve.wait_ge(rstd_wide, 2)
            for m in range(KC):
                nc.vector.scalar_tensor_tensor(x[:, m, :], x[:, m, :], gains[:, G_FINAL + m, :], ps[6][:],
                                               ALU.mult, ALU.mult).then_inc(fin_done, 1)

        @block.tensor
        def _(pe):
            def product(out, a_hi, a_lo, b_hi, b_lo, first, last):
                nc.tensor.matmul(out, a_hi, b_hi, start=first, stop=False)
                nc.tensor.matmul(out, a_hi, b_lo, start=False, stop=False)
                return nc.tensor.matmul(out, a_lo, b_hi, start=False, stop=last)

            def tile_of(slot, w, bank, order=range(KC), wait=None, base=0, hidden_g=None):
                m_hi, m_lo = hidden_g or (h_hi, h_lo)
                for pos, k in enumerate(order):
                    if wait is not None:
                        pe.wait_ge(wait, base + pos + 1)
                    col = (w * KC + k) * P if hidden_g is None else k * P
                    last = product(ps[bank][:], w_hi[slot][:, col:col + P], w_lo[slot][:, col:col + P],
                                   m_hi[:, k, :], m_lo[:, k, :], pos == 0, pos == len(order) - 1)
                last.then_inc(tile_done, 1)

            def channel_sums(n, bank, squares):
                nc.tensor.matmul(ps[bank][:], ones, squares, start=True, stop=True).then_inc(sums_done, 1)

            def ffn(layer, base, tbase, g_hi, g_lo, gate, prod, norm_diag):
                gb = FT * (layer // 2)
                for kind, u0, t0, n, a in ffn_phases(base, tbase):
                    def up(i, j, first=False):
                        if first and layer == 0:
                            pe.wait_ge(first_split, 1)
                        else:
                            pe.wait_ge(w_split, u0 + j + 1 + 2 * i)
                        for w in range(2):
                            if w and first and layer == 0:
                                pe.wait_ge(w_split, 1)
                            t = t0 + 4 * i + 2 * j + w
                            pe.wait_ge(tile_out, t + BANK_CREDIT - 3)
                            tile_of((u0 + j) % 2, w, 2 * j + w, wait=h_ready if first and w == 0 else None,
                                    base=12 * layer)
                            if first and w == 0 and layer:
                                pe.wait_ge(sq_added, 9 * layer)
                                pe.wait_ge(tile_out, BANK_CREDIT + t0)
                                channel_sums(NORM[layer], 6, sumsq[:])
                        if first and layer == 0:
                            pe.wait_ge(const_landed, 32)
                            pe.wait_ge(first_sum, KC // 2 - 1)
                            nc.tensor.matmul(ps[6][:], ones, sumsq[:], start=True, stop=False)
                            pe.wait_ge(pool_step, KC - 1)
                            nc.tensor.matmul(ps[6][:], ones, rope_s[:], start=False, stop=True).then_inc(sums_done, 1)

                    def down(i, j, first=False):
                        t = t0 + 2 * i + j
                        pe.wait_ge(w_split, u0 + j + 1 + 2 * i)
                        pe.wait_ge(tile_out, t + BANK_CREDIT - 1)
                        tile_of((u0 + j) % 2, 0, 4 + j, order=range(parts[a]), wait=g_ready if first else None,
                                base=gb + a, hidden_g=(g_hi, g_lo))

                    step = up if kind == "up" else down
                    step(0, 0, first=kind == "down" or a == 0)
                    step(0, 1)
                    with pe.Fori(1, n // 2) as i:
                        for j in range(2):
                            step(i, j)

            parts = {a: b - a for a, b in PARTS}
            ffn(0, 0, 0, *ffn_mem[1])

            pe.wait_ge(w_split, U_MIX + 1)
            pe.wait_ge(tile_out, BANK_CREDIT + T_MIX - 1)
            tile_of(U_MIX % 2, 0, 4, wait=h_ready, base=8)
            pe.wait_ge(sq_added, 9)
            channel_sums(1, 6, sumsq[:])
            for t in range(ST):
                last = nc.tensor.matmul(ps[7][:, t:t + 1], sumsq[:, t * P:(t + 1) * P], ones[:, 0:1],
                                        start=True, stop=True)
            last.then_inc(sums_done, 1)
            U, T = U_MIX, T_MIX

            def project(unit, t, n_before):
                pe.wait_ge(w_split, U + unit + 1)
                pe.wait_ge(tile_out, BANK_CREDIT + n_before + 1)
                for w in range(2):
                    tile_of((U + unit) % 2, w, 2 * ((unit + 1) % 2) + w)

            def project_values(unit, half, banks, free):
                slot = (U + unit) % 2
                pe.wait_ge(w_split, U + unit + 1)
                for t in range(ST):
                    if half == 0:
                        free(t)
                    tok = slice(t * P, (t + 1) * P)
                    for k in range(4):
                        c = 4 * half + k
                        cols = slice(k * S, (k + 1) * S)
                        last = product(ps[banks[t]][:], h_hi[:, c, tok], h_lo[:, c, tok],
                                       w_hi[slot][:, cols], w_lo[slot][:, cols], c == 0, c == KC - 1)
                    if half:
                        last.then_inc(tile_done, 1)
                if half == 0:
                    last.then_inc(v_half, 1)

            def gla_scores(g, bank):
                p, r = g // 2, GLA_DK * (g % 2)
                for t in range(ST):
                    tok = slice(t * P, (t + 1) * P)
                    last = nc.tensor.matmul(ps[bank][:, tok], projT[r:r + GLA_DK, T_GK + p, tok],
                                            projT[r:r + GLA_DK, T_GQ + p, tok], start=True, stop=True)
                last.then_inc(ag_done, 1)

            def gla_adds():
                pe.wait_ge(tile_out, BANK_CREDIT + T + 13)
                pe.wait_ge(ktail_out, 2)
                for c in range(NCH - 1):
                    rows = slice(CHUNK * (c % 2), CHUNK * (c % 2) + CHUNK)
                    for p in range(2):
                        for hh in range(2):
                            g = 2 * p + hh
                            last = nc.tensor.matmul(
                                ps[4 + 2 * p + c % 2][hh * GLA_DK:(hh + 1) * GLA_DK, (c // 2) * P:(c // 2 + 1) * P],
                                k_tok[p][rows, c // 2, hh * GLA_DK:(hh + 1) * GLA_DK],
                                v_gla[rows, c // 2, g * P:(g + 1) * P], start=True, stop=True)
                        last.then_inc(u_done, 1)

            def gla_output(g):
                p, r = g // 2, GLA_DK * (g % 2)
                pe.wait_ge(ag_out, g + 1)
                pe.wait_ge(state_done, 2 * (NCH - 1))
                for t in range(ST):
                    tok = slice(t * P, (t + 1) * P)
                    nc.tensor.matmul(ps[4 + g][:, tok], v_gla[:, t, g * P:(g + 1) * P], att_g[g][:, tok],
                                     start=t == 0, stop=False, skip_group_check=True)
                for c in range(1, NCH):
                    tok = slice(c * CHUNK, (c + 1) * CHUNK)
                    last = nc.tensor.matmul(ps[4 + g][:, tok], state[p][r:r + GLA_DK, c, :],
                                            projT[r:r + GLA_DK, T_GQ + p, tok],
                                            start=False, stop=c == NCH - 1, skip_group_check=True)
                last.then_inc(og_done, 1)

            project(1, T + 1, T - 1)
            pe.wait_ge(tile_out, BANK_CREDIT + T + 1)
            for p in range(2):
                nc.tensor.matmul(ps[5 - p][:], wa2[:, p * P:(p + 1) * P], projT[0:GLA_RANK, T_GA, :],
                                 start=True, stop=True).then_inc(z_done, 1)
            project(2, T + 3, T - 1)
            project(3, T + 5, T + 2)
            project(4, T + 7, T + 4)
            project_values(5, 0, (4, 5, 6, 7), lambda t: pe.wait_ge(*((z_out, 2 - t) if t < 2 else (sums_out, t))))
            pe.wait_ge(tile_out, BANK_CREDIT + T + 9)
            for p in range(2):
                pe.wait_ge(gla_ready, 3 * p + 1)
                for t in range(ST):
                    last = nc.tensor.transpose(ps[p][:, t * P:(t + 1) * P], gt[1][p][:, t * P:(t + 1) * P], ident)
                last.then_inc(ktail_done, 1)
            pe.wait_ge(gla_ready, 3)
            gla_scores(0, 2)
            gla_scores(1, 3)
            project_values(6, 1, (4, 5, 6, 7), None)
            pe.wait_ge(gla_ready, 6)
            pe.wait_ge(ktail_out, 2)
            gla_scores(2, 0)
            gla_scores(3, 1)
            project_values(7, 0, (2, 3, 0, 1), lambda t: pe.wait_ge(ag_out, t + 1))
            gla_adds()
            project_values(8, 1, (2, 3, 0, 1), None)
            for g in range(GLA_H):
                gla_output(g)
            project(9, T + 17, T + 16)

            def scores(h, i):
                q = 4 * h + i
                r = HD * (h % 2)
                if i == 0:
                    pe.wait_ge(rope_done, 2 * (h // 2) + 2)
                if q >= 2:
                    pe.wait_ge(s_masked, q - 1)
                else:
                    pe.wait_ge(gla_ln, q + 1)
                nc.tensor.matmul(ps[4 + i % 2][:, 0:(i + 1) * P], projT[r:r + HD, T_AQ + 2 * (h // 2), i * P:(i + 1) * P],
                                 projT[r:r + HD, T_AK + 2 * (h // 2), 0:(i + 1) * P], start=True, stop=True).then_inc(s_done, 1)

            def transpose_probs(h, i):
                q = 4 * h + i
                off = P * i * (i + 1) // 2
                pe.wait_ge(diag_done, q + 1)
                if h:
                    pe.wait_ge(pt_out, q - 3)
                else:
                    pe.wait_ge(tile_out, BANK_CREDIT + T + (23 if i < 2 else 25))
                for j in range(i + 1):
                    last = nc.tensor.matmul(ps[i][:, j * P:(j + 1) * P], probs[h % 2][:, off + j * P:off + (j + 1) * P],
                                            diag[:, q % NDIAG, :], start=True, stop=True)
                last.then_inc(pt_done, 1)

            def weigh_values(h):
                r = HD * (h % 2)
                pe.wait_ge(pt_out, 4 * h + 4)
                if h >= 2:
                    pe.wait_ge(o_out, h - 1)
                else:
                    pe.wait_ge(gla_ln, 4)
                for j in range(ST):
                    last = nc.tensor.matmul(ps[6 + h % 2][r:r + HD, j * P:S], v_att[:, j, h * HD:(h + 1) * HD],
                                            probsT[h % 2][:, j, j * P:S], start=j == 0, stop=j == ST - 1)
                last.then_inc(o_done, 1)

            for g in range(GLA_H):
                pe.wait_ge(og_squared, g + 1)
                nc.tensor.matmul(ps[4 + g][:], ones, sq_gla[g], start=True, stop=True).then_inc(gla_sums_done, 1)
            project(10, T + 19, T + 16)
            scores(0, 0)
            scores(0, 1)
            project(11, T + 21, T + 18)
            scores(0, 2)
            scores(0, 3)
            pe.wait_ge(w_split, U + 13)
            pe.wait_ge(tile_out, BANK_CREDIT + T + 21)
            tile_of((U + 12) % 2, 0, 2)
            scores(1, 0)
            scores(1, 1)
            tile_of((U + 12) % 2, 1, 3)
            for h in range(ATT_H):
                for i in range(4):
                    q = 4 * h + i + AHEAD
                    if q < 4 * ATT_H:
                        scores(q // 4, q % 4)
                    transpose_probs(h, i)
                    if i == 1 and h:
                        weigh_values(h - 1)

            UO, TO = U + 13, T + 25

            def token_sums(bank, squares):
                for t in range(ST):
                    last = nc.tensor.matmul(ps[bank][:, t:t + 1], squares[:, t * P:(t + 1) * P], ones[:, 0:1],
                                            start=True, stop=True)
                last.then_inc(sums_done, 1)

            def spread(n, bank, diags):
                pe.wait_ge(norm_diag_done, ST * (n + 1))
                for t in range(ST):
                    last = nc.tensor.matmul(ps[bank][:, t * P:(t + 1) * P], ones, diags[:, t, :], start=True, stop=True)
                last.then_inc(rstd_wide, 1)

            def half_tile(m, chunks, first, last_of_tile, wait_base=None):
                w, slot = m % 2, (UO + m // 2) % 2
                for k in chunks:
                    if wait_base is not None:
                        pe.wait_ge(h_ready, wait_base + k + 1)
                    col = (w * KC + k) * P
                    ins = product(ps[m % 4][:], w_hi[slot][:, col:col + P], w_lo[slot][:, col:col + P],
                                  h_hi[:, k, :], h_lo[:, k, :], first and k == chunks[0],
                                  last_of_tile and k == chunks[-1])
                    if m == KC - 1 and k < KC - 1:
                        ins.then_inc(h_free, 1)
                if last_of_tile:
                    ins.then_inc(tile_done, 1)

            for m in range(4):
                pe.wait_ge(w_split, UO + m // 2 + 1)
                pe.wait_ge(pt_out, 4 * ATT_H - 3 + m)
                half_tile(m, range(4), True, False, 16 if m == 0 else None)
                if m == 0:
                    weigh_values(ATT_H - 1)
                if m == 1:
                    pe.wait_ge(att_squares, 4)
                    token_sums(4, rope_s[:])
                if m == 2:
                    spread(0, 5, diag)
            for m in range(4):
                half_tile(m, range(4, 8), False, True, 16 if m == 0 else None)
            for m in range(4, KC):
                pe.wait_ge(w_split, UO + m // 2 + 1)
                pe.wait_ge(tile_out, BANK_CREDIT + TO + m - 3)
                half_tile(m, range(KC), True, True)
            ffn(2, U_FFN2, T_FFN2, *ffn_mem[2])
            pe.wait_ge(sq_added, 9 * 2 + KC)
            pe.wait_ge(sq_done, 8 * 3)
            for t in range(ST):
                tok = slice(t * P, (t + 1) * P)
                nc.tensor.matmul(ps[7][:, t:t + 1], sumsq[:, tok], ones[:, 0:1], start=True, stop=False)
                last = nc.tensor.matmul(ps[7][:, t:t + 1], square[:, tok], ones[:, 0:1], start=False, stop=True)
            last.then_inc(sums_done, 1)
            spread(1, 6, ffn_mem[2][4])


def _constants():
    c = np.zeros((P, N_CONST), np.float32)
    row = np.arange(P)
    c[:, C_ID:C_ID + P] = np.eye(P)
    c[:, C_ONE:C_ONE + P] = 1.0
    dist = (S - P + row)[:, None] - np.arange(S)[None, :]
    seen = sum(((dist >= 0) & (dist % d == 0) & (dist // d <= w // d)).astype(np.float64) for w, d in PATTERNS)
    c[:, C_STRIP:C_STRIP + S] = np.where(seen > 0, np.log(np.maximum(seen, 1)) / SCORE_SCALE, FAR)
    tri = (row[:, None] // CHUNK == row[None, :] // CHUNK) & (row[:, None] <= row[None, :])
    c[:, C_TRI:C_TRI + S] = np.tile(tri, (1, ST))
    c[:, C_SCAN:C_SCAN + S] = (np.arange(S) % CHUNK != 0)[None, :]
    dim = row % HD
    freq = np.float32(THETA) ** (-np.arange(0, ROT, 2, dtype=np.float32) / np.float32(ROT))
    c[:, C_FREQ] = np.where(dim < ROT, freq[dim % (ROT // 2)], 0.0)
    c[:, C_EPS] = EPS
    c[:, C_SGN] = np.where(dim < ROT // 2, -1.0, np.where(dim < ROT, 1.0, 0.0))
    return c


def _blocks(w, width=P):
    k, n = w.shape
    return w.reshape(k // P, P, n // width, width).transpose(2, 1, 0, 3).reshape(n // width, P, k // P * width)


def kernel(x, positions, ffn1_norm, ffn1_w1, ffn1_w3, ffn1_w2, mix_norm, w_in, gla_w_a2, gla_b_a, gla_out_norm,
           att_out_norm, w_out, ffn2_norm, ffn2_w1, ffn2_w3, ffn2_w2, final_norm):
    import concourse.bacc as bacc
    from concourse.bass_utils import run_bass_kernel_spmd

    def col(v):
        return np.asarray(v).reshape(-1, P).T

    def ffn(w1, w3, w2):
        up = np.concatenate([_blocks(np.asarray(w1)[0]), _blocks(np.asarray(w3)[0])], axis=2)
        w2 = np.asarray(w2)[0]
        return up, [_blocks(w2[a * P:b * P]) for a, b in PARTS]

    def pairs(b):
        n, p, w = b.shape
        return b.reshape(n // 2, 2, p, w).transpose(0, 2, 1, 3).reshape(n // 2, p, 2 * w)

    def values(w):
        return w.reshape(2, 4, P, S).transpose(0, 2, 1, 3).reshape(2, P, 4 * S)

    w = np.asarray(w_in)[0]
    up1, (d1a, d1b) = ffn(ffn1_w1, ffn1_w3, ffn1_w2)
    up2, (d2a, d2b) = ffn(ffn2_w1, ffn2_w3, ffn2_w2)
    arrays = {
        "xT": np.asarray(x)[0].T.reshape(KC, P, S),
        "positions": np.asarray(positions).reshape(1, S),
        "gains": np.concatenate([col(v) for v in (ffn1_norm, mix_norm, ffn2_norm, final_norm, gla_out_norm,
                                                  att_out_norm, gla_b_a)], axis=1),
        "up1": up1, "down1a": d1a, "down1b": d1b,
        "w_proj": pairs(np.concatenate([_blocks(w[:, c:c + n]) for c, n in
                                        [(GQ, GLA_KW), (GK, GLA_KW), (GR, GLA_W)] +
                                        [(c + P * n, P) for n in range(4) for c in (AQ, AK)]])),
        "w_ga": _blocks(w[:, GA:GA + P])[0],
        "w_v": np.concatenate([values(w[:, GV:GV + GLA_W]), values(w[:, AV:AV + ATT_W])]),
        "w_a2": np.asarray(gla_w_a2)[0],
        "w_o": pairs(_blocks(np.asarray(w_out)[0])),
        "up2": up2, "down2a": d2a, "down2b": d2b,
        "const": _constants(),
    }
    arrays = {k: np.ascontiguousarray(v) for k, v in arrays.items()}
    nc = bacc.Bacc("TRN2", target_bir_lowering=False, num_devices=1)
    ap = {k: nc.dram_tensor("in_" + k, v.shape, mybir.dt.from_np(v.dtype), kind="ExternalInput").ap() for k, v in arrays.items()}
    outT = nc.dram_tensor("outT", (KC, P, S), F32, kind="ExternalOutput").ap()
    layer_program(nc, ap["xT"], ap["positions"], ap["gains"], ap["up1"], (ap["down1a"], ap["down1b"]), ap["w_proj"],
                  ap["w_ga"], ap["w_v"], ap["w_a2"], ap["w_o"], ap["up2"], (ap["down2a"], ap["down2b"]),
                  ap["const"], outT)
    r = run_bass_kernel_spmd(nc, [{"in_" + k: v for k, v in arrays.items()}], core_ids=[0])
    return r.results[0]["outT"].reshape(D, S).T.reshape(1, S, D)
```
